# Optimizing a Trainium2 kernel written in Bass

```python
import math
import jax
import jax.numpy as jnp
from jax import lax
import numpy as np

D_MODEL = 1024
BATCH = 1
SEQ = 512
DEPTH = 2
DEC_BATCH = 1
DEC_SEQ = 32
PAST_LEN = 128

CHUNK = 64
N_PAIRS = DEPTH // 2
EPS = 1e-6
NEG_INF = -1e30
ROPE_THETA = 500000.0
HEAD_DIM = 64
ROT_DIM = HEAD_DIM // 4
Q_BLOCK = 128

POOL_WINDOWS = (2, 4, 8, 16)
POOL_GROUP = D_MODEL // 8
D_A = len(POOL_WINDOWS) * POOL_GROUP
POOL_STATE = max(POOL_WINDOWS) - 1

H_B = D_MODEL // 128
HKV_B = 2
GQA_B = H_B // HKV_B
WINDOW = 128
WIN_CHUNKS = WINDOW // CHUNK
D_B = H_B * HEAD_DIM
D_EVEN_IN = D_A + D_B + 2 * HKV_B * HEAD_DIM

H_C = 4
DK_C = 64
DV_C = 128
GATE_RANK = 16
GATE_NORM = 16.0
D_CQK = H_C * DK_C
D_C = H_C * DV_C

H_D = 4
HD_D = 64
D_D = H_D * 2 * HD_D
D_ODD_IN = 2 * D_CQK + 2 * D_C + GATE_RANK + 3 * D_D

D_FF = 2816
CONV_W = 3

kernel_name = 'hybrid_streaming_encoder_step'

def rms_norm(x, w):
    xf = x.astype(jnp.float32)
    y = xf * lax.rsqrt(jnp.mean(xf * xf, axis=-1, keepdims=True) + EPS)
    return (y * w.astype(jnp.float32)).astype(x.dtype)

def rope_partial(x, pos):
    half = ROT_DIM // 2
    inv = jnp.exp(-math.log(ROPE_THETA) * jnp.arange(half, dtype=jnp.float32) * (2.0 / ROT_DIM))
    ang = pos.astype(jnp.float32)[:, None] * inv[None, :]
    shape = (1, pos.shape[0]) + (1,) * (x.ndim - 3) + (half,)
    cos = jnp.cos(ang).reshape(shape)
    sin = jnp.sin(ang).reshape(shape)
    xr = x[..., :ROT_DIM].astype(jnp.float32)
    x1, x2 = xr[..., :half], xr[..., half:]
    rot = jnp.concatenate([x1 * cos - x2 * sin, x2 * cos + x1 * sin], axis=-1)
    return jnp.concatenate([rot.astype(x.dtype), x[..., ROT_DIM:]], axis=-1)

def sink_softmax(s, sink):
    sink = sink.astype(jnp.float32)
    m = jnp.maximum(jnp.max(s, axis=-1, keepdims=True), sink)
    e = jnp.exp(s - m)
    return e / (jnp.sum(e, axis=-1, keepdims=True) + jnp.exp(sink - m))

def pool_mixer(u, prev, pos, w_pool, scale):
    b, l, _ = u.shape
    ext = jnp.concatenate([prev.astype(u.dtype), u], axis=1).astype(jnp.float32)
    csum = jnp.concatenate([jnp.zeros((b, 1, D_A), jnp.float32), jnp.cumsum(ext, axis=1)], axis=1)
    base = POOL_STATE + 1
    outs = []
    for g, w in enumerate(POOL_WINDOWS):
        lo, hi = g * POOL_GROUP, (g + 1) * POOL_GROUP
        total = csum[:, base:base + l, lo:hi] - csum[:, base - w:base - w + l, lo:hi]
        count = jnp.minimum(w, pos + 1).astype(jnp.float32)[None, :, None]
        diff = total / count - ext[:, POOL_STATE:, lo:hi]
        outs.append(jnp.einsum('blc,cd->bld', diff, w_pool[g].astype(jnp.float32)))
    y = jnp.concatenate(outs, axis=-1) * scale.astype(jnp.float32)
    return y.astype(u.dtype), ext[:, -POOL_STATE:].astype(u.dtype)

def swa_prompt(q, k, v, sinks):
    b, s = q.shape[:2]
    nc = s // CHUNK
    scale = HEAD_DIM ** -0.5
    qc = q.reshape(b, nc, CHUNK, HKV_B, GQA_B, HEAD_DIM)

    def banded(t):
        tc = t.reshape(b, nc, CHUNK, HKV_B, HEAD_DIM)
        tp = jnp.concatenate([jnp.zeros((b, WIN_CHUNKS) + tc.shape[2:], t.dtype), tc], axis=1)
        return jnp.concatenate([tp[:, j:j + nc] for j in range(WIN_CHUNKS + 1)], axis=2)

    kb, vb = banded(k), banded(v)
    src_chunk = jnp.arange(nc)[:, None] - WIN_CHUNKS + jnp.repeat(jnp.arange(WIN_CHUNKS + 1), CHUNK)[None, :]
    valid = src_chunk >= 0
    sc = jnp.einsum('bnqhgd,bnkhd->bnhgqk', qc, kb).astype(jnp.float32) * scale
    sc = jnp.where(valid[None, :, None, None, None, :], sc, NEG_INF)
    p = sink_softmax(sc, sinks.reshape(HKV_B, GQA_B)[None, None, :, :, None, None])
    o = jnp.einsum('bnhgqk,bnkhd->bnqhgd', p.astype(v.dtype), vb)
    return o.reshape(b, s, D_B)

def swa_sample(q, k, v, k_cache, v_cache, sinks):
    b, l = q.shape[:2]
    scale = HEAD_DIM ** -0.5
    k_all = jnp.concatenate([k_cache.astype(k.dtype), k], axis=1)
    v_all = jnp.concatenate([v_cache.astype(v.dtype), v], axis=1)
    qg = q.reshape(b, l, HKV_B, GQA_B, HEAD_DIM)
    sc = jnp.einsum('bqhgd,bkhd->bhgqk', qg, k_all).astype(jnp.float32) * scale
    p = sink_softmax(sc, sinks.reshape(HKV_B, GQA_B)[None, :, :, None, None])
    o = jnp.einsum('bhgqk,bkhd->bqhgd', p.astype(v.dtype), v_all).reshape(b, l, D_B)
    rows = k_cache.shape[1]
    return o, k_all[:, -rows:], v_all[:, -rows:]

def even_mixer(h, pos, prompt, pool_prev, swa_k_c, swa_v_c, w_in, w_pool, pool_scale, sinks, w_out):
    b, l, _ = h.shape
    z = h @ w_in
    u, q, k, v = jnp.split(z, [D_A, D_A + D_B, D_A + D_B + HKV_B * HEAD_DIM], axis=-1)
    ya, pool_new = pool_mixer(u, pool_prev, pos, w_pool, pool_scale)
    q = rope_partial(q.reshape(b, l, H_B, HEAD_DIM), pos)
    k = rope_partial(k.reshape(b, l, HKV_B, HEAD_DIM), pos)
    v = v.reshape(b, l, HKV_B, HEAD_DIM)
    if prompt:
        yb = swa_prompt(q, k, v, sinks)
        k_new, v_new = k[:, -WINDOW:], v[:, -WINDOW:]
    else:
        yb, k_new, v_new = swa_sample(q, k, v, swa_k_c, swa_v_c, sinks)
    y = jnp.concatenate([ya, yb], axis=-1) @ w_out
    return y, pool_new, k_new, v_new

def gla_chunked(q, k, v, log_a, s0):
    b, l, h, dk = q.shape
    dv = v.shape[-1]
    blk = min(CHUNK, l)
    n = l // blk

    def split(t):
        return t.reshape(b, n, blk, h, t.shape[-1]).transpose(1, 0, 3, 2, 4)

    causal = jnp.tril(jnp.ones((blk, blk), dtype=bool))

    def step(state, inp):
        qb, kb, vb, gb = inp
        cum = jnp.cumsum(gb, axis=2)
        q_dec = qb * jnp.exp(cum)
        k_dec = kb * jnp.exp(-cum)
        att = jnp.where(causal, jnp.einsum('bhqd,bhkd->bhqk', q_dec, k_dec), 0.0)
        out = jnp.einsum('bhqk,bhkv->bhqv', att, vb) + jnp.einsum('bhqd,bhdv->bhqv', q_dec, state)
        last = cum[:, :, -1:, :]
        new_state = (jnp.exp(last[:, :, 0, :])[..., None] * state
                     + jnp.einsum('bhkd,bhkv->bhdv', kb * jnp.exp(last - cum), vb))
        return new_state, out

    s_fin, o = lax.scan(step, s0, (split(q), split(k), split(v), split(log_a)))
    return o.transpose(1, 0, 3, 2, 4).reshape(b, l, h, dv), s_fin

def diff_prompt(q, k, v, lam):
    b, s = q.shape[:2]
    nb = s // Q_BLOCK
    scale = HD_D ** -0.5
    qb = q.reshape(b, nb, Q_BLOCK, H_D, 2, HD_D).transpose(1, 0, 2, 3, 4, 5)
    key_chunk = jnp.arange(s) // CHUNK

    def one_block(args):
        qi, i = args
        sc = jnp.einsum('bqhcd,bkhcd->bhcqk', qi, k).astype(jnp.float32) * scale
        q_chunk = (i * Q_BLOCK + jnp.arange(Q_BLOCK)) // CHUNK
        mask = key_chunk[None, :] <= q_chunk[:, None]
        p = jax.nn.softmax(jnp.where(mask, sc, NEG_INF), axis=-1)
        a = p[:, :, 0] - lam * p[:, :, 1]
        return jnp.einsum('bhqk,bkhv->bqhv', a.astype(v.dtype), v)

    o = lax.map(one_block, (qb, jnp.arange(nb)))
    return o.transpose(1, 0, 2, 3, 4).reshape(b, s, H_D, 2 * HD_D)

def diff_sample(q, k, v, k_cache, v_cache, lam):
    scale = HD_D ** -0.5
    k_all = jnp.concatenate([k_cache.astype(k.dtype), k], axis=1)
    v_all = jnp.concatenate([v_cache.astype(v.dtype), v], axis=1)
    sc = jnp.einsum('bqhcd,bkhcd->bhcqk', q, k_all).astype(jnp.float32) * scale
    p = jax.nn.softmax(sc, axis=-1)
    a = p[:, :, 0] - lam * p[:, :, 1]
    return jnp.einsum('bhqk,bkhv->bqhv', a.astype(v.dtype), v_all)

def odd_mixer(h, pos, prompt, s_prev, diff_k_c, diff_v_c, w_in, w_gate2, b_gate, gla_norm_w,
              lam_params, diff_norm_w, w_out, lambda_init):
    b, l, _ = h.shape
    f32 = jnp.float32
    z = h @ w_in
    i1 = D_CQK
    i2 = i1 + D_CQK
    i3 = i2 + D_C
    i4 = i3 + D_C
    i5 = i4 + GATE_RANK
    i6 = i5 + D_D
    i7 = i6 + D_D
    cq, ck, cv, cg, cr, dq, dk, dvv = jnp.split(z, [i1, i2, i3, i4, i5, i6, i7], axis=-1)
    log_a = jax.nn.log_sigmoid((cr @ w_gate2 + b_gate).astype(f32)) / GATE_NORM
    qg = cq.reshape(b, l, H_C, DK_C).astype(f32) * (DK_C ** -0.5)
    kg = ck.reshape(b, l, H_C, DK_C).astype(f32)
    vg = cv.reshape(b, l, H_C, DV_C).astype(f32)
    og, s_new = gla_chunked(qg, kg, vg, log_a.reshape(b, l, H_C, DK_C), s_prev.astype(f32))
    og = rms_norm(og, gla_norm_w)
    yc = (og.reshape(b, l, D_C) * jax.nn.silu(cg.astype(f32))).astype(h.dtype)
    q = rope_partial(dq.reshape(b, l, H_D, 2, HD_D), pos)
    k = rope_partial(dk.reshape(b, l, H_D, 2, HD_D), pos)
    v = dvv.reshape(b, l, H_D, 2 * HD_D)
    lp = lam_params.astype(f32)
    lam = jnp.exp(jnp.sum(lp[0] * lp[1])) - jnp.exp(jnp.sum(lp[2] * lp[3])) + lambda_init
    if prompt:
        od = diff_prompt(q, k, v, lam)
    else:
        od = diff_sample(q, k, v, diff_k_c, diff_v_c, lam)
    od = rms_norm(od, diff_norm_w) * (1.0 - lambda_init)
    yd = od.reshape(b, l, D_D).astype(h.dtype)
    y = jnp.concatenate([yc, yd], axis=-1) @ w_out
    return y, s_new.astype(h.dtype), k, v

def conv_ffn(h, conv_prev, w_up, conv_w, conv_b, w_down):
    b, l, _ = h.shape
    gate, val = jnp.split(h @ w_up, 2, axis=-1)
    ext = jnp.concatenate([conv_prev.astype(h.dtype), gate], axis=1)
    conv = conv_b
    for j in range(CONV_W):
        conv = conv + ext[:, j:j + l] * conv_w[j]
    y = (jax.nn.gelu(conv) * val) @ w_down
    return y, ext[:, -(CONV_W - 1):]

def trunk(x, pos, prompt, cache_pool, cache_swa_k, cache_swa_v, state_gla, cache_diff_k, cache_diff_v,
          cache_ffn_conv, norm_mix_w, norm_ffn_w, final_norm_w, even_w_in, pool_w, pool_scale, swa_sinks,
          even_w_out, odd_w_in, gla_w_gate2, gla_b_gate, gla_norm_w, diff_lambda, diff_norm_w, odd_w_out,
          ffn_w_up, ffn_conv_w, ffn_conv_b, ffn_w_down):
    b = x.shape[0]
    pools, swa_ks, swa_vs, glas, diff_ks, diff_vs, ffns = [], [], [], [], [], [], []
    for layer in range(DEPTH):
        p = layer // 2
        h = rms_norm(x, norm_mix_w[layer])
        if layer % 2 == 0:
            pool_prev = jnp.zeros((b, POOL_STATE, D_A), x.dtype) if prompt else cache_pool[p]
            y, pool_new, k_new, v_new = even_mixer(
                h, pos, prompt, pool_prev,
                None if prompt else cache_swa_k[p], None if prompt else cache_swa_v[p],
                even_w_in[p], pool_w[p], pool_scale[p], swa_sinks[p], even_w_out[p])
            pools.append(pool_new)
            swa_ks.append(k_new)
            swa_vs.append(v_new)
        else:
            s_prev = jnp.zeros((b, H_C, DK_C, DV_C), jnp.float32) if prompt else state_gla[p]
            lambda_init = 0.8 - 0.6 * math.exp(-0.3 * layer)
            y, s_new, k_new, v_new = odd_mixer(
                h, pos, prompt, s_prev,
                None if prompt else cache_diff_k[p], None if prompt else cache_diff_v[p],
                odd_w_in[p], gla_w_gate2[p], gla_b_gate[p], gla_norm_w[p], diff_lambda[p],
                diff_norm_w[p], odd_w_out[p], lambda_init)
            glas.append(s_new)
            diff_ks.append(k_new)
            diff_vs.append(v_new)
        x = x + y
        h = rms_norm(x, norm_ffn_w[layer])
        conv_prev = jnp.zeros((b, CONV_W - 1, D_FF), x.dtype) if prompt else cache_ffn_conv[layer]
        y, conv_new = conv_ffn(h, conv_prev, ffn_w_up[layer], ffn_conv_w[layer], ffn_conv_b[layer], ffn_w_down[layer])
        ffns.append(conv_new)
        x = x + y
    return (rms_norm(x, final_norm_w), jnp.stack(pools), jnp.stack(swa_ks), jnp.stack(swa_vs),
            jnp.stack(glas), jnp.stack(diff_ks), jnp.stack(diff_vs), jnp.stack(ffns))

def setup_inputs(seed: int = 0) -> dict:
    key = jax.random.key(seed)
    ks = iter(list(jax.random.split(key, 32)))

    def nrm(shape, scale):
        return scale * jax.random.normal(next(ks), shape, jnp.float32)

    def gain(shape):
        return 1.0 + 0.05 * jax.random.normal(next(ks), shape, jnp.float32)

    swa_rows = min(WINDOW, PAST_LEN)
    return {
        'x_prompt': nrm((BATCH, SEQ, D_MODEL), 1.0),
        'x_sample': nrm((DEC_BATCH, DEC_SEQ, D_MODEL), 1.0),
        'cache_pool': nrm((N_PAIRS, DEC_BATCH, POOL_STATE, D_A), 1.0),
        'cache_swa_k': nrm((N_PAIRS, DEC_BATCH, swa_rows, HKV_B, HEAD_DIM), 1.0),
        'cache_swa_v': nrm((N_PAIRS, DEC_BATCH, swa_rows, HKV_B, HEAD_DIM), 1.0),
        'state_gla': nrm((N_PAIRS, DEC_BATCH, H_C, DK_C, DV_C), 0.5),
        'cache_diff_k': nrm((N_PAIRS, DEC_BATCH, PAST_LEN, H_D, 2, HD_D), 1.0),
        'cache_diff_v': nrm((N_PAIRS, DEC_BATCH, PAST_LEN, H_D, 2 * HD_D), 1.0),
        'cache_ffn_conv': nrm((DEPTH, DEC_BATCH, CONV_W - 1, D_FF), 1.0),
        'norm_mix_w': gain((DEPTH, D_MODEL)),
        'norm_ffn_w': gain((DEPTH, D_MODEL)),
        'final_norm_w': gain((D_MODEL,)),
        'even_w_in': nrm((N_PAIRS, D_MODEL, D_EVEN_IN), D_MODEL ** -0.5),
        'pool_w': nrm((N_PAIRS, len(POOL_WINDOWS), POOL_GROUP, POOL_GROUP), POOL_GROUP ** -0.5),
        'pool_scale': gain((N_PAIRS, D_A)),
        'swa_sinks': nrm((N_PAIRS, H_B), 1.0),
        'even_w_out': nrm((N_PAIRS, D_A + D_B, D_MODEL), (D_A + D_B) ** -0.5),
        'odd_w_in': nrm((N_PAIRS, D_MODEL, D_ODD_IN), D_MODEL ** -0.5),
        'gla_w_gate2': nrm((N_PAIRS, GATE_RANK, D_CQK), GATE_RANK ** -0.5),
        'gla_b_gate': nrm((N_PAIRS, D_CQK), 0.1),
        'gla_norm_w': gain((N_PAIRS, DV_C)),
        'diff_lambda': nrm((N_PAIRS, 4, HD_D), 0.1),
        'diff_norm_w': gain((N_PAIRS, 2 * HD_D)),
        'odd_w_out': nrm((N_PAIRS, D_C + D_D, D_MODEL), (D_C + D_D) ** -0.5),
        'ffn_w_up': nrm((DEPTH, D_MODEL, 2 * D_FF), D_MODEL ** -0.5),
        'ffn_conv_w': nrm((DEPTH, CONV_W, D_FF), 0.5),
        'ffn_conv_b': nrm((DEPTH, D_FF), 0.02),
        'ffn_w_down': nrm((DEPTH, D_FF, D_MODEL), D_FF ** -0.5),
    }

def reference(x_prompt, x_sample, cache_pool, cache_swa_k, cache_swa_v, state_gla, cache_diff_k, cache_diff_v,
              cache_ffn_conv, norm_mix_w, norm_ffn_w, final_norm_w, even_w_in, pool_w, pool_scale, swa_sinks,
              even_w_out, odd_w_in, gla_w_gate2, gla_b_gate, gla_norm_w, diff_lambda, diff_norm_w, odd_w_out,
              ffn_w_up, ffn_conv_w, ffn_conv_b, ffn_w_down):
    weights = (norm_mix_w, norm_ffn_w, final_norm_w, even_w_in, pool_w, pool_scale, swa_sinks, even_w_out,
               odd_w_in, gla_w_gate2, gla_b_gate, gla_norm_w, diff_lambda, diff_norm_w, odd_w_out,
               ffn_w_up, ffn_conv_w, ffn_conv_b, ffn_w_down)
    pos_p = jnp.arange(x_prompt.shape[1])
    pos_s = PAST_LEN + jnp.arange(x_sample.shape[1])
    (y_prompt, new_pool_p, new_swa_k_p, new_swa_v_p, new_gla_p, new_diff_k_p, new_diff_v_p,
     new_ffn_p) = trunk(x_prompt, pos_p, True, None, None, None, None, None, None, None, *weights)
    (y_sample, new_pool_s, new_swa_k_s, new_swa_v_s, new_gla_s, new_diff_k_s, new_diff_v_s,
     new_ffn_s) = trunk(x_sample, pos_s, False, cache_pool, cache_swa_k, cache_swa_v, state_gla,
                        cache_diff_k, cache_diff_v, cache_ffn_conv, *weights)
    return (y_prompt, y_sample,
            new_pool_p, new_swa_k_p, new_swa_v_p, new_gla_p, new_diff_k_p, new_diff_v_p, new_ffn_p,
            new_pool_s, new_swa_k_s, new_swa_v_s, new_gla_s, new_diff_k_s, new_diff_v_s, new_ffn_s)


_drawn_inputs = setup_inputs


def setup_inputs(seed=0):
    import zlib

    import numpy as np

    out = dict(_drawn_inputs(seed))
    spreads = {}
    factors = {'swa_sinks': 8.0, 'gla_norm_w': 3.62, 'diff_norm_w': 3.914, 'ffn_conv_b': 3.719}
    for name, (base, spread) in spreads.items():
        noise = np.random.default_rng([zlib.crc32(name.encode()), seed]).standard_normal(out[name].shape)
        drawn = base * np.exp(spread * noise) if base else spread * noise
        out[name] = jnp.asarray(drawn.astype(out[name].dtype))
    for name, factor in factors.items():
        out[name] = (out[name] * factor).astype(out[name].dtype)
    return out
```

```python
import math
from contextlib import ExitStack

import concourse.bass as bass
import numpy as np
from concourse import mybir

F32 = mybir.dt.float32
F32R = mybir.dt.float32r
BF16 = mybir.dt.bfloat16
ALU = mybir.AluOpType
ACT = mybir.ActivationFunctionType
AX = mybir.AxisListType

P = 128
D, SEQ, SMP, PAST = 1024, 512, 32, 128
T = SEQ + SMP
HALF = T // 2
KC = D // P
FF = 2816
FC = FF // P
CHUNK = 64
EPS = 1e-6
NEG = -1e30
LAMBDA_INIT = 0.8 - 0.6 * math.exp(-0.3 * 1)
POOL_W = (2, 4, 8, 16)
PS = 15
UE = PS + SEQ + PS + SMP
GE = 2 + SEQ + 2 + SMP
CO = SEQ + 2 + SMP
KEYS = SEQ + PAST + SMP
THETA, ROT = 500000.0, 16

EVEN_IN, ODD_IN, OUT, UP, DOWN_PARTS = 10, 25, 8, 2 * FC, 3
DOWN = KC * DOWN_PARTS
S_EVEN_OUT = EVEN_IN
S_UP = [EVEN_IN + OUT, 0]
S_DOWN = [S_UP[0] + UP, 0]
S_ODD_IN = S_DOWN[0] + DOWN
S_ODD_OUT = S_ODD_IN + ODD_IN
S_UP[1] = S_ODD_OUT + OUT
S_DOWN[1] = S_UP[1] + UP
NSLAB = S_DOWN[1] + DOWN
RING, RAW = 4, 2

COLS = {}
_at = 0
for _name, _n in (("ident", 128), ("ones", 128), ("causal", 128), ("norm", 5 * KC), ("conv_w", 2 * FC * 3),
                  ("conv_b", 2 * FC), ("conv_past", 2 * FC * 2), ("pool_scale", 4), ("sinks", 8),
                  ("b_gate", 2), ("gla_norm", 1), ("diff_norm", 1), ("eps", 1), ("inv_count", 64)):
    COLS[_name] = (_at, _at + _n)
    _at += _n
NCONST = _at

ODD_CHUNKS = (["cr"] + ["cq"] * 2 + ["ck"] * 2 + ["cv"] * 4 + ["dv"] * 4 + ["cg"] * 4 + ["dk"] * 4 + ["dq"] * 4)
EVEN_CHUNKS = ["u"] * 4 + ["v", "k"] + ["q"] * 4
V_KW0, V_ALL = 9, 11
T_STATES = [2, 4, 6, 8, 9]
X_ODD = 3 * KC
NEVEN, NODD, NOUT = 5, 4, 23
PARTNER = [(k + 8) % 16 if k < 16 else k for k in range(32)]
GLA_SLOT0 = 14
TILES = [(t * P, P if t < 4 else SMP) for t in range(5)]


def build(nc, io):
    ctx = ExitStack()
    with ctx:
        base = 16512
        top = [base]

        def at(name, shape, dt, offset):
            return nc.alloc_sbuf_tensor_at(name, shape, dt, offset=offset)

        def sb(name, shape, dt=F32):
            size = int(np.prod(shape[1:])) * (2 if dt == BF16 else 4)
            size = (size + 31) // 32 * 32
            t = at(name, shape, dt, top[0])
            top[0] += size
            return t

        x = sb("x", [P, KC, T])
        h_at = top[0]
        h_hi = sb("h_hi", [P, KC, T], F32R)
        h_lo_at = top[0]
        h_lo = sb("h_lo", [P, KC, T], F32R)
        y_at = top[0]
        y_hi = sb("y_hi", [P, FC, T], F32R)
        y_lo_at = top[0]
        y_lo = sb("y_lo", [P, FC, T], F32R)
        w_hi = sb("w_hi", [P, RING, 1024], F32R)
        w_lo = sb("w_lo", [P, RING, 1024], F32R)
        w_raw = sb("w_raw", [P, RAW, 1024])
        sumsq = sb("sumsq", [P, T])
        rstd = sb("rstd", [P, T])
        sq_at = top[0]
        sq = sb("sq", [P, 2, T])
        ffn_at = top[0]
        gate = [sb(f"gate{p}", [P, GE]) for p in range(2)]
        conv = [sb(f"conv{p}", [P, CO]) for p in range(2)]
        consts = sb("consts", [P, NCONST])
        tails = sb("tails", [P, FC, 4])
        mask_q = sb("mask_q", [P, 2, P], BF16)
        mask_k = sb("mask_k", [P, CHUNK], BF16)
        small = sb("small", [P, 2, 24])
        elast = sb("elast", [P, 2, 9])
        lam = sb("lam", [P, 8])
        tick = sb("tick", [1, 1])
        dnorm = sb("dnorm", [P, 1])
        assert top[0] <= nc.sbuf_usable_end, (top[0], nc.sbuf_usable_end)

        def const(name, *shape):
            a, b = COLS[name]
            v = consts[:, a:b]
            if len(shape) == 2:
                v = v.rearrange("p (a b) -> p a b", a=shape[0])
            if len(shape) == 3:
                v = v.rearrange("p (a b c) -> p a b c", a=shape[0], b=shape[1])
            return v

        ident, ones, causal = const("ident"), const("ones"), const("causal")
        norm_w = const("norm", 5, KC)
        conv_w, conv_b, conv_past = const("conv_w", 2, FC, 3), const("conv_b", 2, FC), const("conv_past", 2, FC, 2)
        eps = const("eps")

        def region(prefix, start, end):
            here = [start]

            def take(name, shape):
                t = at(prefix + name, shape, F32, here[0])
                here[0] += (int(np.prod(shape[1:])) * 4 + 31) // 32 * 32
                assert here[0] <= end, name
                return t
            return take

        r1 = region("even_", y_at + 4 * T * 4, y_lo_at)
        r2 = region("even_", y_lo_at + 4 * T * 4, y_lo_at + FC * T * 4)
        ez = r1("z", [P, 2, T])
        e_vT = r1("vT", [P, T])
        e_v = r1("v", [P, 5, P])
        e_kT = r1("kT", [P, KEYS])
        e_qT = r1("qT", [P, 4, T])
        e_u = r1("u", [P, 4, UE])
        e_wpool = r1("wpool", [P, 4, P])
        e_vc = r1("vc", [P, P])
        e_rope = r1("rope", [P, 2, T])
        e_w = r2("winsum", [P, 2, UE])
        e_diff = r2("diff", [P, 4, T])
        e_swap = r2("rope_swapped", [P, T])

        r1 = region("odd_", y_at + 4 * T * 4, y_lo_at)
        r2 = region("odd_", y_lo_at + 4 * T * 4, y_lo_at + FC * T * 4)
        oz = r1("z", [P, 2, T])
        o_cr = r1("cr", [P, T])
        o_swap = at("odd_rope_swapped", [P, T], F32, y_at + 4 * T * 4 + 2 * T * 4)
        o_wg = r1("wgate_then_state", [P, 256])
        o_q = r1("gla_q", [P, 2, T])
        o_k = r1("gla_k", [P, 2, T])
        o_kd = r1("gla_kd", [P, 2, T])
        o_sg = r1("silu", [P, 4, T])
        o_rope = r1("rope", [P, 2, T])
        o_st = r1("states", [P, 4, 256])
        o_lp = r1("lambda_in", [P, 256])
        o_cv = r2("cv", [P, 5, 512])
        o_dv = r2("dv", [P, 5, 512])
        o_kw = r2("kw", [P, 5, 256])
        dk_at = y_lo_at + 4 * T * 4 + (2 * 2560 + 1280) * 4
        d_kT = r2("kT", [P, 4, KEYS])
        d_vc = r2("vc", [P, 512])
        gate_tmp = [at("gate_tmp0", [P, 4, T], F32, dk_at), at("gate_tmp1", [P, 4, T], F32, ffn_at)]
        d_qT = at("d_qT", [P, 4, T], F32, ffn_at)
        probs = [at(f"probs{b}", [P, 1024], F32, h_at + b * 4096) for b in range(2)]
        probsT = [at(f"probsT{b}", [P, 2, 512], F32, h_lo_at + b * 4096) for b in range(2)]
        att_m = at("att_masked", [P, 512], F32, sq_at)
        head_t = at("head_tmp", [P, 512], F32, sq_at + 2048)
        sq_h, r_h = sumsq[:, 0:512], rstd[:, 0:512]
        o_s_in = sb("sample_state", [P, 256])
        o_s_out = o_wg

        psum = ctx.enter_context(nc.psum_tensor("psum", [P, 8, 512], F32))

        def pair(k):
            return psum[:, 2 * k:2 * k + 2, 0:HALF]

        def pieces(k):
            return [(psum[:, 2 * k, 0:HALF], 0, HALF),
                    (psum[:, 2 * k + 1, 0:SEQ - HALF], HALF, SEQ - HALF),
                    (psum[:, 2 * k + 1, SEQ - HALF:HALF], SEQ, SMP)]

        def halves(v):
            return v.rearrange("p (h t) -> p h t", h=2)

        def sem(name):
            return ctx.enter_context(nc.semaphore(name))

        in_x, in_const = sem("in_x"), sem("in_const")
        in_even, in_odd = sem("in_even"), sem("in_odd")
        in_w = [sem(f"in_w{r}") for r in range(RAW)]
        out_done = sem("out_done")
        ticks = sem("ticks")
        w_hi_done, w_ready = sem("w_hi_done"), sem("w_ready")
        slab_done, mid_done = sem("slab_done"), sem("mid_done")
        sum_ready = sem("sum_ready")
        turned, side_mm = sem("turned"), sem("side_mm")
        s_ready, p_turned, o_ready = sem("s_ready"), sem("p_turned"), sem("o_ready")
        att_ready, og_ready = sem("att_ready"), sem("og_ready")
        head_sum = sem("head_sum")
        act, vec = sem("act"), sem("vec")
        sq_ready, rms_ready, h_hi_done = sem("sq_ready"), sem("rms_ready"), sem("h_hi_done")
        evac = sem("evac")
        v_out = sem("v_out")
        e_ready, pT_out, y_hi_done = sem("e_ready"), sem("pT_out"), sem("y_hi_done")
        gate_l, decays = sem("gate_l"), sem("decays")
        gate_out, gelu_ready, ffn_hi = sem("gate_out"), sem("gelu_ready"), sem("ffn_hi")
        hsq_ready, hrms_ready = sem("hsq_ready"), sem("hrms_ready")
        setup = sem("setup")
        sum_add, h_f, h_ready = sem("sum_add"), sem("h_f"), sem("h_ready")
        x_upd = sem("x_upd")
        rope_done, diff_ready = sem("rope_done"), sem("diff_ready")
        y_lo_done = sem("y_lo_done")
        negm, p_norm = sem("negm"), sem("p_norm")
        gate_z, cum_ready, gla_in = sem("gate_z"), sem("cum_ready"), sem("gla_in")
        att_out, st_ready = sem("att_out"), sem("st_ready")
        og_read, head_y = sem("og_read"), sem("head_y")
        conv_ready, y_f, y_ready = sem("conv_ready"), sem("y_f"), sem("y_ready")
        lam_sum, lam_exp = sem("lam_sum"), sem("lam_exp")
        in_cache = sem("in_cache")
        y_out = sem("y_out")

        EU = [(b, g) for b in range(5) for g in range(2)]
        OU = [(b, h) for b in range(5) for h in range(4)]

        def even_block(b):
            if b == 4:
                return (SEQ, SMP), (SEQ, PAST + SMP), [("cache", P), (4, SMP)]
            lo = max(b - 1, 0)
            return (b * P, P), (lo * P, (b + 1 - lo) * P), [(t, P) for t in range(lo, b + 1)]

        def odd_block(b):
            if b == 4:
                return (SEQ, SMP), (SEQ, PAST + SMP), [("cache", P), (4, SMP)]
            return (b * P, P), (0, (b + 1) * P), [(t, P) for t in range(b + 1)]

        def s_even(u):
            b = u % 2
            return psum[:, 2 * b:2 * b + 2, :].rearrange("p c (h k) -> p (c h) k", h=2)

        class Order:

            def __init__(self, eng, own):
                self.eng, self.own, self.n = eng, own, {}
                self.last = None

            def __call__(self, ins, sem_=None):
                s = self.own if sem_ is None else sem_
                ins.then_inc(s, 1)
                self.n[s.name] = self.n.get(s.name, 0) + 1
                self.last = (s, self.n[s.name])
                return self.n[s.name]

            def wait(self):
                self.eng.wait_ge(*self.last)

        def settle(eng):
            eng.wait_ge(in_const, 16)

        block = ctx.enter_context(nc.Block())

        @block.sync
        def _(sp):
            sp.dma_start(x[:, :, :], io["x"]).then_inc(in_x, 16)

            def load(s, r):
                sp.dma_start(w_raw[:, r], io["weights"][s]).then_inc(in_w[r], 16)

            for s in range(RAW):
                load(s, s)
            for s in range(RAW, RING):
                sp.wait_ge(w_ready, s - RAW + 1)
                load(s, s % RAW)
            with sp.Fori(1, NSLAB // RING) as i:
                for k in range(RING):
                    sp.wait_ge(w_ready, RING * i + (k - RAW + 1))
                    load(RING * i + k, k % RAW)
            for s in range(NSLAB // RING * RING, NSLAB):
                sp.wait_ge(w_ready, s - RAW + 1)
                load(s, s % RAW)
            for c in range(KC):
                sp.wait_ge(y_out, c + 1)
                sp.dma_start(io["y"][:, c * T:(c + 1) * T], x[:, c]).then_inc(out_done, 16)
            sp.wait_ge(out_done, 16 * NOUT)

        @block.gpsimd
        def _(pool):
            pool.memset(tick[:, :], 0.0).then_inc(ticks, 1)

            def split(i, k, first=False):
                s = RING * i + k
                pool.wait_ge(in_w[k % RAW], (RING // RAW) * 16 * i + 16 * (k // RAW + 1))
                if not first:
                    pool.wait_ge(ticks, 1)
                    pool.wait_ge(slab_done, s - RING + 1)
                    pool.tensor_tensor(tick[:, :], tick[:, :], tick[:, :], ALU.mult).then_inc(ticks, 1)
                pool.tensor_scalar(w_hi[:, k], w_raw[:, k % RAW], 1.0, 0.0, ALU.mult, ALU.add).then_inc(w_hi_done, 1)
                pool.wait_ge(w_hi_done, s + 1)
                pool.tensor_tensor(w_lo[:, k], w_raw[:, k % RAW], w_hi[:, k].bitcast(F32),
                                   ALU.subtract).then_inc(w_ready, 1)

            for k in range(RING):
                split(0, k, first=True)
            with pool.Fori(1, NSLAB // RING) as i:
                for k in range(RING):
                    split(i, k)
            for s in range(NSLAB // RING * RING, NSLAB):
                split(s // RING, s % RING)

        @block.tensor
        def _(pe):
            def tiles(acc, s, pairs, first, last):
                for n, (kt, xh, xl) in enumerate(pairs):
                    wh = w_hi[:, s % RING, kt * P:(kt + 1) * P]
                    wl = w_lo[:, s % RING, kt * P:(kt + 1) * P]
                    for half in range(2):
                        cols = slice(half * HALF, (half + 1) * HALF)
                        out = psum[:, 2 * acc + half, 0:HALF]
                        pe.matmul(out, wh, xh[:, cols], start=first and n == 0, stop=False)
                        pe.matmul(out, wh, xl[:, cols], start=False, stop=False)
                        ins = pe.matmul(out, wl, xh[:, cols], start=False, stop=last and n == len(pairs) - 1)
                return ins

            def h_tiles(c0, c1):
                return [(c, h_hi[:, c], h_lo[:, c]) for c in range(c0, c1)]

            def total(n, acc):
                pe.wait_ge(sum_add, KC * (n + 1))
                for half in range(2):
                    ins = pe.matmul(psum[:, 2 * acc + half, 0:HALF], ones, sumsq[:, half * HALF:(half + 1) * HALF],
                                    start=True, stop=True)
                ins.then_inc(sum_ready, 1)

            def in_projection(n_norm, s0, ev0, chunks, side):
                for n in range(chunks):
                    pe.wait_ge(w_ready, s0 + n + 1)
                    if n >= 2:
                        pe.wait_ge(evac, ev0 + n - 1)
                    for c in range(KC):
                        if n == 0:
                            pe.wait_ge(h_ready, KC * n_norm + c + 1)
                        ins = tiles(2 + n % 2, s0 + n, h_tiles(c, c + 1), c == 0, c == KC - 1)
                    ins.then_inc(slab_done, 1)
                    side(n)

            def out_chunk(s, m, acc, yh, yl, c0):
                pe.wait_ge(w_ready, s + 1)
                part = [(4 * (m % 2) + c, yh[:, c0 + c], yl[:, c0 + c]) for c in range(4)]
                tiles(acc, s, part, True, True).then_inc(slab_done if m % 2 else mid_done, 1)

            def ffn(layer, n_norm, upd0):
                s0, d0, f0 = S_UP[layer], S_DOWN[layer], FC * layer

                def up(i, k, fresh=False):
                    pe.wait_ge(w_ready, RING * i + (s0 + k + 1))
                    if not fresh:
                        pe.wait_ge(y_f if k % 2 else gate_out, 2 * i + (f0 + k // 2 - 1))
                    tiles(k, s0 + k, h_tiles(0, KC), True, True).then_inc(slab_done, 1)

                pe.wait_ge(w_ready, s0 + 2)
                for c in range(KC):
                    pe.wait_ge(h_ready, KC * n_norm + c + 1)
                    for k in range(2):
                        ins = tiles(k, s0 + k, h_tiles(c, c + 1), c == 0, c == KC - 1)
                        if c == KC - 1:
                            ins.then_inc(slab_done, 1)
                for k in range(2, RING):
                    up(0, k, fresh=True)
                with pe.Fori(1, FC // 2) as i:
                    for k in range(RING):
                        up(i, k)

                def down(i, j):
                    for part in range(DOWN_PARTS):
                        k = DOWN_PARTS * j + part
                        pe.wait_ge(w_ready, 4 * DOWN_PARTS * i + (d0 + k + 1))
                        lo, hi = 8 * part, min(8 * part + 8, FC)
                        if part == 0:
                            pe.wait_ge(x_upd, 4 * i + (upd0 + j - 1))
                            if j < 2:
                                pe.wait_ge(y_f, f0 + FC - 1)
                        for f in range(lo, hi):
                            if j == 0:
                                pe.wait_ge(y_ready, f0 + f + 1)
                            ins = tiles(j % 2, d0 + k, [(f - lo, y_hi[:, f], y_lo[:, f])], f == 0, f == FC - 1)
                        ins.then_inc(slab_done, 1)

                with pe.Fori(0, 2) as i:
                    for j in range(4):
                        down(i, j)

            pe.wait_ge(in_const, 16)
            pe.wait_ge(setup, 1)
            total(0, 0)

            def even_side(n):
                if n == 5:
                    pe.wait_ge(evac, 5)
                    pe.wait_ge(rms_ready, 1)
                    for t, (c, w) in enumerate(TILES):
                        ins = pe.transpose(psum[0:w, t // 4, (t % 4) * P:(t % 4 + 1) * P], e_vT[:, c:c + w], ident)
                    ins.then_inc(turned, 1)
                if n >= 6:
                    g = n - 6
                    if g == 0:
                        pe.wait_ge(in_even, 16 * NEVEN)
                    pe.wait_ge(diff_ready, g + 1)
                    if g == 1:
                        pe.wait_ge(v_out, 1)
                    if g >= 2:
                        pe.wait_ge(y_lo_done, g - 1)
                    acc = (g + 1) % 2
                    for half in range(2):
                        ins = pe.matmul(psum[:, 2 * acc + half, 0:HALF], e_wpool[:, g],
                                        e_diff[:, g, half * HALF:(half + 1) * HALF], start=True, stop=True)
                    ins.then_inc(side_mm, 1)

            in_projection(0, 0, 0, EVEN_IN, even_side)

            def even_scores(u):
                b, g = EU[u]
                (q0, nq), (k0, nk), _ = even_block(b)
                if u < 2:
                    pe.wait_ge(rope_done, 5)
                    pe.wait_ge(y_lo_done, 4)
                else:
                    pe.wait_ge(pT_out, u - 1)
                rows = slice(64 * g, 64 * g + 64)
                S = s_even(u)
                for j in range(4):
                    ins = pe.matmul(S[0:nq, j, 0:nk], e_qT[rows, j, q0:q0 + nq], e_kT[rows, k0:k0 + nk],
                                    start=True, stop=b == 4)
                    if b < 4:
                        ins = pe.matmul(S[0:nq, j, nk - CHUNK:nk], mask_q[rows, 0], mask_k[rows],
                                        start=False, stop=b == 0)
                    if 0 < b < 4:
                        ins = pe.matmul(S[0:nq, j, 0:CHUNK], mask_q[rows, 1], mask_k[rows], start=False, stop=True)
                ins.then_inc(s_ready, 1)

            even_scores(0)
            even_scores(1)
            for u, (b, g) in enumerate(EU):
                (q0, nq), _, runs = even_block(b)
                pe.wait_ge(p_norm, u + 1)
                pr = probs[u % 2][:, :].rearrange("p (h k) -> p h k", h=4)
                for kb, (_, kn) in enumerate(runs):
                    for j in range(4):
                        ins = pe.transpose(psum[0:kn, 2 * (u % 2) + kb, j * nq:(j + 1) * nq],
                                           pr[0:nq, j, kb * P:kb * P + kn], ident[0:nq, 0:nq])
                ins.then_inc(p_turned, 1)
                if u < KC:
                    if u >= 1:
                        pe.wait_ge(x_upd, u)
                    else:
                        pe.wait_ge(evac, EVEN_IN)
                    out_chunk(S_EVEN_OUT + u // 2, u, 3, y_hi, y_lo, 0)
                pe.wait_ge(pT_out, u + 1)
                if g == 0 and b >= 1:
                    pe.wait_ge(y_lo_done, 4 + b)
                for kb, (t, kn) in enumerate(runs):
                    v = e_vc[0:kn, 64 * g:64 * g + 64] if t == "cache" else e_v[0:kn, t, 64 * g:64 * g + 64]
                    ins = pe.matmul(psum[64 * g:64 * g + 64, 4, 0:4 * nq], v, probsT[u % 2][0:kn, kb, 0:4 * nq],
                                    start=kb == 0, stop=kb == len(runs) - 1)
                ins.then_inc(o_ready, 1)
                if u + 2 < len(EU):
                    even_scores(u + 2)
            pe.wait_ge(y_lo_done, 9)
            for m in range(KC):
                pe.wait_ge(x_upd, KC + m - 1)
                out_chunk(S_EVEN_OUT + 4 + m // 2, m, 2 + m % 2, h_hi, h_lo, 4)
            total(1, 0)
            pe.wait_ge(x_upd, 2 * KC)
            ffn(0, 1, 2 * KC)
            total(2, 2)

            def turn(n, src, waits):
                for s, v in waits:
                    pe.wait_ge(s, v)
                for t, (c, w) in enumerate(TILES):
                    ins = pe.transpose(psum[0:w, t // 4, (t % 4) * P:(t % 4 + 1) * P], src[:, c:c + w], ident)
                ins.then_inc(turned, 1)

            def odd_side(n):
                if n == 1:
                    pe.wait_ge(in_odd, 16 * NODD)
                    pe.wait_ge(evac, EVEN_IN + 1)
                    for j in range(2):
                        for half in range(2):
                            ins = pe.matmul(psum[:, 2 * j + half, 0:HALF], o_wg[0:16, j * P:(j + 1) * P],
                                            o_cr[0:16, half * HALF:(half + 1) * HALF], start=True, stop=True)
                    ins.then_inc(side_mm, 1)
                if 6 <= n < 14:
                    waits = [(evac, EVEN_IN + n)]
                    waits += [(v_out, 1 + n - 6)] if n > 6 else [(gate_z, 2)]
                    turn(n, oz[:, (n - 1) % 2], waits)
                if n == 12:
                    pe.wait_ge(gla_in, 2)
                    for t in range(4):
                        for j in range(2):
                            ins = pe.transpose(psum[:, 2 + t // 2, (2 * (t % 2) + j) * P:(2 * (t % 2) + j + 1) * P],
                                               o_k[:, j, t * P:(t + 1) * P], ident)
                    ins.then_inc(side_mm, 1)
                if n == 13:
                    pe.wait_ge(v_out, V_KW0)
                    for j in range(2):
                        ins = pe.transpose(psum[0:SMP, 2, j * P:(j + 1) * P], o_k[:, j, SEQ:T], ident)
                    ins.then_inc(side_mm, 1)
                if n >= GLA_SLOT0:
                    k = n - GLA_SLOT0
                    if k % 2 == 0:
                        if k >= 2:
                            t = k // 2 - 1
                            w = TILES[t][1]
                            pe.wait_ge(hsq_ready, t + 1)
                            pe.wait_ge(og_read, t + 1)
                            for p in range(2):
                                ins = pe.matmul(psum[:, 2 + p, 256:256 + 2 * w], ones, sq_h[:, 2 * w * p:2 * w * (p + 1)],
                                                start=True, stop=True)
                            ins.then_inc(head_sum, 1)
                        if k // 2 < 5:
                            stage_a(k // 2)
                    else:
                        stage_b((k - 1) // 2)

            def stage_a(t):
                c0, w = TILES[t]
                if t == 0:
                    pe.wait_ge(v_out, V_ALL)
                else:
                    pe.wait_ge(st_ready, T_STATES[t - 1])
                for j in range(2):
                    for p in range(2):
                        pe.matmul(psum[0:w, p, j * w:(j + 1) * w], o_kd[64 * p:64 * p + 64, j, c0:c0 + w],
                                  o_q[64 * p:64 * p + 64, j, c0:c0 + w], start=True, stop=True)
                for cc in range(2 if t < 4 else 1):
                    r = slice(64 * cc, 64 * cc + min(w, 64))
                    for j in range(2):
                        for p in range(2):
                            e = 2 * p + j
                            ins = pe.matmul(psum[64 * p:64 * p + 64, cc, 256 + j * P:256 + (j + 1) * P],
                                            o_kw[r, t, j * P + 64 * p:j * P + 64 * p + 64],
                                            o_cv[r, t, e * P:(e + 1) * P], start=True, stop=True)
                ins.then_inc(att_ready, 1)

            def stage_b(t):
                c0, w = TILES[t]
                pe.wait_ge(att_out, t + 1)
                pe.wait_ge(st_ready, T_STATES[t] - (1 if t < 4 else 1))
                if t >= 1:
                    pe.wait_ge(head_y, t)
                for p in range(2):
                    for j in range(2):
                        e = 2 * p + j
                        out = psum[:, 2 + p, j * w:(j + 1) * w]
                        pe.matmul(out, o_cv[0:w, t, e * P:(e + 1) * P], att_m[0:w, e * w:(e + 1) * w],
                                  start=True, stop=False)
                        for cc in range(2 if t < 4 else 1):
                            st = o_s_in if t == 4 else o_st[:, (2 * t + cc) % 4]
                            cw = min(w, CHUNK)
                            ins = pe.matmul(out[:, cc * CHUNK:cc * CHUNK + cw],
                                            st[64 * p:64 * p + 64, j * P:(j + 1) * P],
                                            o_q[64 * p:64 * p + 64, j, c0 + cc * CHUNK:c0 + cc * CHUNK + cw],
                                            start=False, stop=(cc == 1 or t == 4))
                ins.then_inc(og_ready, 1)

            in_projection(2, S_ODD_IN, EVEN_IN, ODD_IN, odd_side)

            def odd_scores(u):
                b, h = OU[u]
                (q0, nq), (k0, nk), _ = odd_block(b)
                if u < 2:
                    pe.wait_ge(rope_done, 5 + 8)
                    pe.wait_ge(y_lo_done, 9 + 5)
                    pe.wait_ge(in_cache, 32)
                else:
                    pe.wait_ge(pT_out, 10 + u - 1)
                for c in range(2):
                    rows = slice(64 * c, 64 * c + 64)
                    S = psum[0:nq, 2 * (u % 2) + c, 0:nk]
                    ins = pe.matmul(S, d_qT[rows, h, q0:q0 + nq], d_kT[rows, h, k0:k0 + nk],
                                    start=True, stop=b == 4)
                    if b < 4:
                        ins = pe.matmul(psum[0:nq, 2 * (u % 2) + c, nk - CHUNK:nk], mask_q[rows, 0], mask_k[rows],
                                        start=False, stop=True)
                ins.then_inc(s_ready, 1)

            odd_scores(0)
            odd_scores(1)
            for u, (b, h) in enumerate(OU):
                (q0, nq), _, runs = odd_block(b)
                pe.wait_ge(p_norm, 10 + u + 1)
                for kb, (_, kn) in enumerate(runs):
                    ins = pe.transpose(psum[0:kn, 2 * (u % 2), kb * nq:(kb + 1) * nq],
                                       probs[u % 2][0:nq, kb * P:kb * P + kn], ident[0:nq, 0:nq])
                ins.then_inc(p_turned, 1)
                if u % 2 == 0 and u // 2 < KC:
                    m = u // 2
                    if m >= 1:
                        pe.wait_ge(x_upd, X_ODD + m)
                    else:
                        pe.wait_ge(evac, EVEN_IN + ODD_IN)
                    out_chunk(S_ODD_OUT + m // 2, m, 3, y_hi, y_lo, 0)
                pe.wait_ge(pT_out, 10 + u + 1)
                if h == 0 and b >= 1:
                    pe.wait_ge(head_y, 5 + b)
                for kb, (t, kn) in enumerate(runs):
                    v = d_vc[0:kn, h * P:(h + 1) * P] if t == "cache" else o_dv[0:kn, t, h * P:(h + 1) * P]
                    ins = pe.matmul(psum[:, 4, h * nq:(h + 1) * nq], v, probsT[u % 2][0:kn, 0, kb * nq:(kb + 1) * nq],
                                    start=kb == 0, stop=kb == len(runs) - 1)
                ins.then_inc(o_ready, 1)
                if u + 2 < len(OU):
                    odd_scores(u + 2)
                if h == 3:
                    pe.wait_ge(hsq_ready, 5 + b + 1)
                    pe.matmul(psum[:, 5, 0:4 * nq], ones, sq_h[:, 0:4 * nq], start=True, stop=True)\
                        .then_inc(head_sum, 1)
            pe.wait_ge(y_lo_done, 9 + 10)
            for m in range(KC):
                pe.wait_ge(x_upd, X_ODD + KC + m - 1)
                out_chunk(S_ODD_OUT + 4 + m // 2, m, 2 + m % 2, h_hi, h_lo, 4)
            total(3, 0)
            pe.wait_ge(x_upd, X_ODD + 2 * KC)
            ffn(1, 3, X_ODD + 2 * KC)
            total(4, 2)

        @block.scalar
        def _(ac):
            o = Order(ac, act)
            loop = [None]

            def square(c, n, i=None):
                if i is not None:
                    settle(ac)
                o(ac.activation(sq[:, c % 2], x[:, c] if i is None else x[:, 4 * i + c], ACT.Square), sq_ready)

            def norm(n, acc):
                ac.wait_ge(sum_ready, n + 1)
                o(ac.activation(halves(rstd), pair(acc), ACT.Sqrt, bias=eps, scale=1.0 / D), rms_ready)
                if n < 4:
                    for c in range(KC):
                        ac.wait_ge(h_f, KC * n + c + 1)
                        o(ac.activation(h_hi[:, c], sq[:, c % 2], ACT.Copy), h_hi_done)

            def group_copy(dst, acc, gap):
                for n, (src, c, w) in enumerate(pieces(acc)):
                    at_ = c + gap + (gap if c >= SEQ else 0)
                    ins = ac.activation(dst[:, at_:at_ + w], src, ACT.Copy)
                return ins

            def dma(dst, src, s):
                ac.dma_start(dst, src).then_inc(s, 16)

            def ffn(layer, n_norm, upd0):
                s0, d0, f0, g0 = S_UP[layer], S_DOWN[layer], FC * layer, KC * n_norm

                def chunk(i, p, fresh=False):
                    f = 2 * i + p
                    ac.wait_ge(slab_done, 4 * i + (s0 + 2 * p + 1))
                    if not fresh:
                        ac.wait_ge(conv_ready, 2 * i + (f0 + p - 1))
                    group_copy(gate[p], 2 * p, 2).then_inc(gate_out, 1)
                    ac.wait_ge(conv_ready, 2 * i + (f0 + p + 1))
                    settle(ac)
                    ac.activation(conv[p][:, :], conv[p][:, :], ACT.Gelu_apprx_tanh,
                                  bias=conv_b[:, layer, f:f + 1] if isinstance(i, int) else
                                  conv_b[:, layer, bass.ds(f, 1)]).then_inc(gelu_ready, 1)
                    ac.wait_ge(y_f, 2 * i + (f0 + p + 1))
                    settle(ac)
                    ac.activation(y_hi[:, f, 0:SEQ], conv[p][:, 0:SEQ], ACT.Copy)
                    ac.activation(y_hi[:, f, SEQ:T], conv[p][:, SEQ + 2:CO], ACT.Copy).then_inc(ffn_hi, 1)

                for p in range(2):
                    chunk(0, p, fresh=layer == 0)
                with ac.Fori(1, FC // 2) as i:
                    for p in range(2):
                        chunk(i, p)
                with ac.Fori(0, 2) as i:
                    for j in range(4):
                        ac.wait_ge(x_upd, 4 * i + (upd0 + j + 1))
                        ac.wait_ge(sum_add, 4 * i + (g0 + KC + j - 1))
                        square(j, n_norm + 1, i)

            def out_squares(n, upd0):
                for m in range(KC):
                    ac.wait_ge(x_upd, upd0 + m + 1)
                    ac.wait_ge(sum_add, KC * n + m - 1)
                    square(m, n)

            dma(consts[:, :], io["consts"], in_const)
            dma(e_wpool[:, :, :], io["pool_w"], in_even)
            dma(e_vc[:, :], io["swa_v"], in_even)
            dma(e_rope[:, :, :], io["rope"], in_even)
            dma(e_kT[:, SEQ:SEQ + PAST], io["swa_k"], in_even)
            dma(e_u[:, :, PS + SEQ:2 * PS + SEQ], io["pool_past"], in_even)
            ac.wait_ge(in_x, 16)
            for c in range(KC):
                if c >= 2:
                    ac.wait_ge(sum_add, c - 1)
                square(c, 0)
            ac.wait_ge(in_const, 16)
            norm(0, 0)

            for n, kind in enumerate(EVEN_CHUNKS):
                ac.wait_ge(slab_done, n + 1)
                acc = 2 + n % 2
                if kind == "u":
                    group_copy(e_u[:, n], acc, PS).then_inc(evac, 1)
                elif kind == "v":
                    ac.activation(halves(e_vT[:, :]), pair(acc), ACT.Copy).then_inc(evac, 1)
                else:
                    if n >= 7:
                        ac.wait_ge(rope_done, n - 6)
                    ac.activation(halves(ez[:, n % 2]), pair(acc), ACT.Copy).then_inc(evac, 1)
                if n == 5:
                    ac.wait_ge(turned, 1)
                    ac.activation(e_v[:, 0:4], psum[:, 0, :].rearrange("p (t f) -> p t f", t=4), ACT.Copy)
                    ac.activation(e_v[0:SMP, 4], psum[0:SMP, 1, 0:P], ACT.Copy).then_inc(v_out, 1)
                if n >= 6:
                    g = n - 6
                    ac.wait_ge(side_mm, g + 1)
                    ac.activation(halves(y_hi[:, g]), pair((g + 1) % 2), ACT.Copy,
                                  scale=const("pool_scale")[:, g:g + 1]).then_inc(y_hi_done, 1)
            dma(io["pool_new"][:, :, 0], e_u[:, :, SEQ:SEQ + PS], out_done)
            dma(io["pool_new"][:, :, 1], e_u[:, :, UE - PS:UE], out_done)
            ac.wait_ge(v_out, 1)
            dma(io["swa_v_new"][0], e_v[:, 3], out_done)
            dma(io["swa_v_new"][1, 0:P - SMP], e_vc[SMP:P, :], out_done)
            dma(io["swa_v_new"][1, P - SMP:P], e_v[0:SMP, 4], out_done)
            ac.wait_ge(rope_done, 1)
            dma(io["swa_k_new"][:, 0], e_kT[:, SEQ - P:SEQ], out_done)
            dma(io["swa_k_new"][:, 1], e_kT[:, KEYS - P:KEYS], out_done)

            def even_exp(u):
                b, g = EU[u]
                (_, nq), (_, nk), _ = even_block(b)
                sm = small[0:nq, u % 2]
                ac.wait_ge(negm, u + 1)
                if u >= 2:
                    ac.wait_ge(p_turned, u - 1)
                S = s_even(u)
                for j in range(4):
                    o(ac.activation(probs[u % 2][0:nq, j * 256:j * 256 + nk], S[0:nq, j, 0:nk], ACT.Exp,
                                    bias=sm[:, 4 + j:5 + j], scale=0.125, accum_out=sm[:, 8 + j:9 + j]))
                ac.activation(sm[:, 16:20], sm[:, 12:16], ACT.Exp).then_inc(e_ready, 1)

            even_exp(0)
            for u, (b, g) in enumerate(EU):
                (q0, nq), _, runs = even_block(b)
                if u + 1 < len(EU):
                    even_exp(u + 1)
                ac.wait_ge(p_turned, u + 1)
                if u >= 2:
                    ac.wait_ge(o_ready, u - 1)
                for kb, (_, kn) in enumerate(runs):
                    ins = ac.activation(probsT[u % 2][0:kn, kb, 0:4 * nq], psum[0:kn, 2 * (u % 2) + kb, 0:4 * nq],
                                        ACT.Copy)
                ins.then_inc(pT_out, 1)
                if g == 1:
                    ac.wait_ge(o_ready, u + 1)
                    ac.activation(h_hi[:, 4:8, q0:q0 + nq], psum[:, 4, 0:4 * nq].rearrange("p (j q) -> p j q", j=4),
                                  ACT.Copy).then_inc(y_hi_done, 1)
            out_squares(1, KC)
            norm(1, 0)
            ac.wait_ge(out_done, 16 * 7)
            ffn(0, 1, 2 * KC)

            ac.wait_ge(x_upd, 3 * KC)
            dma(o_wg[0:16, :], io["gate_w"], in_odd)
            dma(o_rope[:, :, :], io["rope"], in_odd)
            dma(o_lp[:, :], io["lambda"], in_odd)
            dma(o_s_in[:, :], io["state"], in_odd)
            dma(io["tails"][:, 0], tails[:, :, :], out_done)
            norm(2, 2)
            for n, kind in enumerate(ODD_CHUNKS):
                ac.wait_ge(slab_done, S_ODD_IN + n + 1)
                acc = 2 + n % 2
                src = pair(acc)
                if kind == "cr":
                    ac.activation(halves(o_cr[0:16, :]), src[0:16], ACT.Copy).then_inc(evac, 1)
                elif kind == "cq":
                    ac.activation(halves(o_q[:, n - 1]), src, ACT.Copy, scale=0.125).then_inc(evac, 1)
                elif kind == "ck":
                    ac.activation(halves(o_k[:, n - 3]), src, ACT.Copy).then_inc(evac, 1)
                elif kind == "cg":
                    ac.activation(halves(o_sg[:, n - 13]), src, ACT.Silu).then_inc(evac, 1)
                else:
                    if 7 <= n < 13:
                        ac.wait_ge(turned, n - 5)
                    elif n in (17, 18):
                        ac.wait_ge(turned, 9)
                    elif n > 18:
                        ac.wait_ge(rope_done, 5 + n - 18)
                    ac.activation(halves(oz[:, n % 2]), src, ACT.Copy).then_inc(evac, 1)
                if n == 0:
                    ac.wait_ge(lam_sum, 1)
                    ac.activation(lam[:, 2:4], lam[:, 0:2], ACT.Exp).then_inc(lam_exp, 1)
                if n == 2:
                    for j in range(2):
                        gt = gate_tmp[j]
                        ac.wait_ge(gate_z, j + 1)
                        o(ac.activation(gt[:, 1], gt[:, 1], ACT.Exp, scale=-1.0))
                        o.wait()
                        ac.activation(gt[:, 1], gt[:, 1], ACT.Ln, bias=1.0).then_inc(gate_l, 1)
                if n == 3:
                    for j in range(2):
                        gt = gate_tmp[j]
                        ac.wait_ge(cum_ready, j + 1)
                        o(ac.activation(gt[:, 0], gt[:, 2], ACT.Exp, scale=1.0 / 16))
                        o(ac.activation(gt[:, 3], gt[:, 2], ACT.Exp, scale=-1.0 / 16))
                        ac.activation(gt[:, 1], gt[:, 1], ACT.Exp, scale=1.0 / 16).then_inc(decays, 1)
                if 6 <= n < 14:
                    dst, h = (o_cv, n - 6) if n < 10 else (o_dv, n - 10)
                    ac.wait_ge(turned, n - 4)
                    o(ac.activation(dst[:, 0:4, h * P:(h + 1) * P],
                                    psum[:, 0, :].rearrange("p (t f) -> p t f", t=4), ACT.Copy))
                    ac.activation(dst[0:SMP, 4, h * P:(h + 1) * P], psum[0:SMP, 1, 0:P], ACT.Copy).then_inc(v_out, 1)
                if n == 12:
                    ac.wait_ge(side_mm, 6)
                    ac.activation(o_kw[:, 0:4].rearrange("p (c t) f -> p c (t f)", c=2), psum[:, 2:4, :], ACT.Copy)\
                        .then_inc(v_out, 1)
                if n == 13:
                    ac.wait_ge(side_mm, 7)
                    ac.activation(o_kw[0:SMP, 4], psum[0:SMP, 2, 0:256], ACT.Copy).then_inc(v_out, 1)
                    ac.wait_ge(v_out, V_ALL)
                    dma(io["diff_v_new"][0:SEQ].rearrange("(t p) f -> p t f", p=P), o_dv[:, 0:4], out_done)
                    dma(io["diff_v_new"][SEQ:T], o_dv[0:SMP, 4], out_done)
                if n >= GLA_SLOT0:
                    k = n - GLA_SLOT0
                    t = (k - 1) // 2
                    if k % 2 == 1:
                        w = TILES[t][1]
                        ac.wait_ge(og_ready, t + 1)
                        if t >= 1:
                            ac.wait_ge(head_sum, t)
                        ac.activation(sq_h[:, 0:4 * w].rearrange("p (c n) -> p c n", c=2), psum[:, 2:4, 0:2 * w],
                                      ACT.Square).then_inc(hsq_ready, 1)
                    elif k >= 2:
                        c0, w = TILES[t]
                        ac.wait_ge(head_sum, t + 1)
                        o(ac.activation(r_h[:, 0:4 * w].rearrange("p (c n) -> p c n", c=2),
                                        psum[:, 2:4, 256:256 + 2 * w], ACT.Ln, bias=eps, scale=1.0 / P))
                        o.wait()
                        ac.activation(r_h[:, 0:4 * w], r_h[:, 0:4 * w], ACT.Exp, scale=-0.5).then_inc(hrms_ready, 1)
                        ac.wait_ge(head_y, t + 1)
                        ac.activation(y_hi[:, 0:4, c0:c0 + w], head_t[:, 0:4 * w].rearrange("p (e q) -> p e q", e=4),
                                      ACT.Copy).then_inc(y_hi_done, 1)
                if n == 14:
                    ac.wait_ge(gla_in, 2)
                    dma(d_kT[:, :, SEQ:SEQ + PAST], io["diff_k"], in_cache)
                    dma(d_vc[:, :], io["diff_v"], in_cache)
            dma(io["state_new"][:, 0], o_st[:, 0], out_done)
            dma(io["state_new"][:, 1], o_s_out[:, :], out_done)
            dma(io["diff_k_new"][:, :, 0:SEQ], d_kT[:, :, 0:SEQ], out_done)
            dma(io["diff_k_new"][:, :, SEQ:T], d_kT[:, :, SEQ + PAST:KEYS], out_done)

            def odd_exp(u):
                b, h = OU[u]
                (_, nq), (_, nk), _ = odd_block(b)
                sm = small[0:nq, u % 2]
                ac.wait_ge(negm, 10 + u + 1)
                if u >= 2:
                    ac.wait_ge(p_turned, 10 + u - 1)
                for c in range(2):
                    ins = ac.activation(probs[u % 2][0:nq, c * 512:c * 512 + nk], psum[0:nq, 2 * (u % 2) + c, 0:nk],
                                        ACT.Exp, bias=sm[:, 4 + c:5 + c], scale=0.125, accum_out=sm[:, 8 + c:9 + c])
                ins.then_inc(e_ready, 1)

            def odd_heads(b):
                (q0, nq), _, _ = odd_block(b)
                ac.wait_ge(head_sum, 5 + b + 1)
                o(ac.activation(r_h[:, 0:4 * nq], psum[:, 5, 0:4 * nq], ACT.Ln, bias=eps, scale=1.0 / P))
                o.wait()
                ac.activation(r_h[:, 0:4 * nq], r_h[:, 0:4 * nq], ACT.Exp, scale=-0.5).then_inc(hrms_ready, 1)
                ac.wait_ge(head_y, 5 + b + 1)
                ac.activation(h_hi[:, 4:8, q0:q0 + nq], head_t[:, 0:4 * nq].rearrange("p (h q) -> p h q", h=4),
                              ACT.Copy).then_inc(y_hi_done, 1)

            odd_exp(0)
            for u, (b, h) in enumerate(OU):
                (q0, nq), _, runs = odd_block(b)
                if u + 1 < len(OU):
                    odd_exp(u + 1)
                ac.wait_ge(p_turned, 10 + u + 1)
                ac.wait_ge(o_ready, 10 + u - 1)
                bank = psum[:, 2 * (u % 2), :]
                if b < 4:
                    n = len(runs) * P
                    ac.activation(probsT[u % 2][:, 0, 0:n], bank[:, 0:n], ACT.Copy).then_inc(pT_out, 1)
                else:
                    ac.activation(probsT[u % 2][:, 0, 0:nq], bank[:, 0:nq], ACT.Copy)
                    ac.activation(probsT[u % 2][0:SMP, 0, nq:2 * nq], bank[0:SMP, nq:2 * nq], ACT.Copy)\
                        .then_inc(pT_out, 1)
                if h == 3:
                    ac.wait_ge(o_ready, 10 + u + 1)
                    ac.wait_ge(head_sum, 5 + b)
                    ac.activation(sq_h[:, 0:4 * nq], psum[:, 4, 0:4 * nq], ACT.Square).then_inc(hsq_ready, 1)
                if h == 0 and b >= 1:
                    odd_heads(b - 1)
            odd_heads(4)
            out_squares(3, X_ODD + KC)
            norm(3, 0)
            ac.wait_ge(out_done, 16 * 14)
            ffn(1, 3, X_ODD + 2 * KC)
            dma(io["tails"][:, 1], tails[:, :, :], out_done)
            norm(4, 2)

        @block.vector
        def _(ve):
            o = Order(ve, vec)

            def clear_sum(n):
                if n:
                    ve.wait_ge(sum_ready, n)
                o(ve.memset(sumsq[:, :], 0.0))

            def add_square(c, n, i=0):
                ve.wait_ge(sq_ready, 4 * i + (KC * n + c + 1))
                ve.tensor_tensor(sumsq[:, :], sumsq[:, :], sq[:, c % 2], ALU.add).then_inc(sum_add, 1)

            def norm(n):
                ve.wait_ge(rms_ready, n + 1)
                o(ve.reciprocal(rstd[:, :], rstd[:, :]))
                o.wait()

                def low(c):
                    ve.wait_ge(h_hi_done, KC * n + c + 1)
                    ve.tensor_tensor(h_lo[:, c], sq[:, c % 2], h_hi[:, c].bitcast(F32), ALU.subtract).then_inc(h_ready, 1)

                for c in range(KC):
                    if c >= 2:
                        ve.wait_ge(h_ready, KC * n + c - 1)
                    ve.scalar_tensor_tensor(sq[:, c % 2], x[:, c], norm_w[:, n, c:c + 1], rstd[:, :],
                                            ALU.mult, ALU.mult).then_inc(h_f, 1)
                    if c:
                        low(c - 1)
                low(KC - 1)

            def add_out(slab, value, acc, m):
                ve.wait_ge(slab, value)
                ve.tensor_tensor(halves(x[:, m]), halves(x[:, m]), pair(acc), ALU.add).then_inc(x_upd, 1)

            def out_first(s0, m, mid0, upd0):
                if m >= 0:
                    add_out(slab_done if m % 2 else mid_done, (s0 if m % 2 else mid0) + m // 2 + 1, 3, m)

            def out_second(s0, mid0, upd0, n):
                for m in range(KC):
                    add_out(slab_done if m % 2 else mid_done, (s0 + 4 if m % 2 else mid0 + 4) + m // 2 + 1, 2 + m % 2, m)
                    add_square(m, n)

            def ffn(layer, n_norm, upd0):
                s0, d0, f0 = S_UP[layer], S_DOWN[layer], FC * layer

                def chunk(i, p):
                    f = 2 * i + p
                    one = slice(f, f + 1) if isinstance(i, int) else bass.ds(f, 1)
                    g, c = gate[p], conv[p]

                    def tap(j):
                        return conv_w[:, layer, one, j]

                    ve.wait_ge(gate_out, 2 * i + (f0 + p + 1))
                    settle(ve)
                    ve.tensor_copy(g[:, SEQ + 2:SEQ + 4].unsqueeze(1), conv_past[:, layer, one, :]).then_inc(vec, 1)
                    ve.tensor_copy(tails[:, one, 0:2], g[:, SEQ:SEQ + 2].unsqueeze(1)).then_inc(vec, 1)
                    ve.tensor_copy(tails[:, one, 2:4], g[:, GE - 2:GE].unsqueeze(1)).then_inc(vec, 1)
                    at_ = 12 * i + (vec0 + 6 * p)
                    ve.wait_ge(vec, at_ + 3)
                    ve.tensor_scalar(c[:, :], g[:, 0:CO], tap(0), None, ALU.mult).then_inc(vec, 1)
                    ve.wait_ge(vec, at_ + 4)
                    ve.scalar_tensor_tensor(c[:, :], g[:, 1:1 + CO], tap(1), c[:, :], ALU.mult, ALU.add)\
                        .then_inc(vec, 1)
                    ve.wait_ge(vec, at_ + 5)
                    ve.scalar_tensor_tensor(c[:, :], g[:, 2:2 + CO], tap(2), c[:, :], ALU.mult, ALU.add)\
                        .then_inc(conv_ready, 1)
                    ve.wait_ge(slab_done, 4 * i + (s0 + 2 * p + 2))
                    ve.wait_ge(gelu_ready, 2 * i + (f0 + p + 1))
                    for n, (src, t0, w) in enumerate(pieces(2 * p + 1)):
                        c0 = t0 + (2 if t0 >= SEQ else 0)
                        ins = ve.tensor_tensor(c[:, c0:c0 + w], c[:, c0:c0 + w], src, ALU.mult)
                    ins.then_inc(y_f, 1)
                    ve.wait_ge(ffn_hi, 2 * i + (f0 + p + 1))
                    ve.tensor_tensor(y_lo[:, f, 0:SEQ], c[:, 0:SEQ], y_hi[:, f, 0:SEQ].bitcast(F32),
                                     ALU.subtract).then_inc(vec, 1)
                    ve.tensor_tensor(y_lo[:, f, SEQ:T], c[:, SEQ + 2:CO], y_hi[:, f, SEQ:T].bitcast(F32),
                                     ALU.subtract).then_inc(y_ready, 1)

                for p in range(2):
                    o(ve.memset(gate[p][:, 0:2], 0.0))
                o.wait()
                vec0 = o.n[vec.name]
                for p in range(2):
                    chunk(0, p)
                with ve.Fori(1, FC // 2) as i:
                    for p in range(2):
                        chunk(i, p)
                o.n[vec.name] += 6 * FC
                clear_sum(n_norm + 1)
                o.wait()
                with ve.Fori(0, 2) as i:
                    for j in range(4):
                        ve.wait_ge(slab_done, 12 * i + (d0 + 3 * j + 3))
                        ve.tensor_tensor(halves(x[:, 4 * i + j]), halves(x[:, 4 * i + j]), pair(j % 2),
                                         ALU.add).then_inc(x_upd, 1)
                        ve.wait_ge(sum_add, 4 * i + (KC * (n_norm + 1) + j))
                        add_square(j, n_norm + 1, i)

            clear_sum(0)
            o(ve.memset(mask_q[:, :, :], 0.0))
            o(ve.memset(mask_k[:, :], 0.0))
            o.wait()
            for r in (0, 64):
                o(ve.memset(mask_q[r:r + 1, 0, 0:CHUNK], 1.0))
                o(ve.memset(mask_q[r:r + 1, 1, CHUNK:P], 1.0))
                o(ve.memset(mask_k[r:r + 1, :], NEG))
            o(ve.memset(e_u[:, :, 0:PS], 0.0))
            ve.nop().then_inc(setup, 1)
            for c in range(KC):
                if c:
                    ve.wait_ge(sum_add, c)
                else:
                    o.wait()
                add_square(c, 0)
            norm(0)

            def rotate(z, swapped, rope, kT, qT_dst):
                o(ve.stream_shuffle(swapped, z, PARTNER))
                o.wait()
                o(ve.tensor_tensor(z, z, rope[:, 0], ALU.mult))
                o(ve.tensor_tensor(swapped, swapped, rope[:, 1], ALU.mult))
                o.wait()
                if kT is None:
                    o(ve.tensor_tensor(qT_dst, z, swapped, ALU.add), rope_done)
                else:
                    o(ve.tensor_tensor(kT[:, 0:SEQ], z[:, 0:SEQ], swapped[:, 0:SEQ], ALU.add))
                    o(ve.tensor_tensor(kT[:, SEQ + PAST:KEYS], z[:, SEQ:T], swapped[:, SEQ:T], ALU.add), rope_done)

            for n in range(EVEN_IN):
                if n < 4:
                    if n == 0:
                        ve.wait_ge(in_even, 16 * NEVEN)
                    ve.wait_ge(evac, n + 1)
                    u, w = e_u[:, n], 1
                    src, k = u, 0
                    while w < POOL_W[n]:
                        dst = e_w[:, k % 2]
                        lo = 2 * w - 1
                        o.wait()
                        o(ve.tensor_tensor(dst[:, lo:UE], src[:, lo:UE], src[:, lo - w:UE - w], ALU.add))
                        src, w, k = dst, 2 * w, k + 1
                    o.wait()
                    o(ve.scalar_tensor_tensor(e_diff[:, n, 0:SEQ], src[:, PS:PS + SEQ], 1.0 / w, u[:, PS:PS + SEQ],
                                              ALU.mult, ALU.subtract))
                    o(ve.scalar_tensor_tensor(e_diff[:, n, SEQ:T], src[:, UE - SMP:UE], 1.0 / w, u[:, UE - SMP:UE],
                                              ALU.mult, ALU.subtract))
                    o.wait()
                    o(ve.tensor_tensor(e_diff[:, n, 0:16], src[:, PS:PS + 16],
                                       const("inv_count")[:, 16 * n:16 * n + 16], ALU.mult))
                    o.wait()
                    o(ve.tensor_tensor(e_diff[:, n, 0:16], e_diff[:, n, 0:16], u[:, PS:PS + 16], ALU.subtract),
                      diff_ready)
                if n >= 5:
                    ve.wait_ge(evac, n + 1)
                    if n > 5:
                        o.wait()
                    rotate(ez[:, n % 2], e_swap[:, :], e_rope, e_kT if n == 5 else None, e_qT[:, max(n - 6, 0)])
                if n >= 6:
                    g = n - 6
                    ve.wait_ge(y_hi_done, g + 1)
                    o(ve.scalar_tensor_tensor(halves(y_lo[:, g]), pair((g + 1) % 2), const("pool_scale")[:, g:g + 1],
                                              halves(y_hi[:, g]).bitcast(F32), ALU.mult, ALU.subtract), y_lo_done)

            def even_max(u):
                b, g = EU[u]
                (_, nq), (_, nk), _ = even_block(b)
                sm = small[0:nq, u % 2]
                sink = const("sinks")[0:nq, 4 * g:4 * g + 4]
                ve.wait_ge(s_ready, u + 1)
                o(ve.tensor_reduce(sm[:, 0:4], s_even(u)[0:nq, :, 0:nk], AX.X, ALU.max))
                o.wait()
                o(ve.scalar_tensor_tensor(sm[:, 0:4], sm[:, 0:4], 0.125, sink, ALU.mult, ALU.max))
                o.wait()
                o(ve.tensor_scalar(sm[:, 4:8], sm[:, 0:4], -1.0, None, ALU.mult))
                o(ve.tensor_tensor(sm[:, 12:16], sink, sm[:, 0:4], ALU.subtract), negm)

            def even_normalise(u):
                b, g = EU[u]
                (_, nq), (_, nk), _ = even_block(b)
                sm = small[0:nq, u % 2]
                ve.wait_ge(e_ready, u + 1)
                o(ve.tensor_tensor(sm[:, 20:24], sm[:, 8:12], sm[:, 16:20], ALU.add))
                o.wait()
                o(ve.reciprocal(sm[:, 20:24], sm[:, 20:24]))
                o.wait()
                pr = probs[u % 2][0:nq, :].rearrange("p (h k) -> p h k", h=4)[:, :, 0:nk]
                o(ve.tensor_tensor(pr, pr, sm[:, 20:24].unsqueeze(2).broadcast_to([nq, 4, nk]), ALU.mult), p_norm)

            def low(b, src):
                (q0, nq), _, _ = odd_block(b)
                o(ve.tensor_tensor(h_lo[:, 4:8, q0:q0 + nq], src, h_hi[:, 4:8, q0:q0 + nq].bitcast(F32),
                                   ALU.subtract), y_lo_done)

            def even_low(b):
                (_, nq), _, _ = even_block(b)
                ve.wait_ge(y_hi_done, 4 + b + 1)
                low(b, psum[:, 4, 0:4 * nq].rearrange("p (j q) -> p j q", j=4))

            even_max(0)
            for u, (b, g) in enumerate(EU):
                if u + 1 < len(EU):
                    even_max(u + 1)
                even_normalise(u)
                if g == 0 and b >= 1:
                    even_low(b - 1)
                if u <= KC:
                    out_first(S_EVEN_OUT, u - 1, 0, 0)
            even_low(4)
            clear_sum(1)
            o.wait()
            for m in range(KC):
                add_out(slab_done if m % 2 else mid_done, (S_EVEN_OUT + 4 if m % 2 else 4) + m // 2 + 1, 2 + m % 2, m)
                ve.wait_ge(sum_add, KC + m)
                add_square(m, 1)
            norm(1)
            ve.wait_ge(out_done, 16 * 7)
            ffn(0, 1, 2 * KC)
            norm(2)

            ve.wait_ge(in_odd, 16 * NODD)
            lp = o_lp[:, :].rearrange("p (a b d) -> p a b d", a=2, b=2)
            o(ve.tensor_tensor(lp[:, :, 0], lp[:, :, 0], lp[:, :, 1], ALU.mult))
            o.wait()
            o(ve.tensor_reduce(lam[:, 0:2], lp[:, :, 0], AX.X, ALU.add), lam_sum)
            o(ve.tensor_scalar(dnorm[:, :], const("diff_norm"), 1.0 - LAMBDA_INIT, None, ALU.mult))
            ve.wait_ge(lam_exp, 1)
            o(ve.tensor_tensor(lam[:, 4:5], lam[:, 2:3], lam[:, 3:4], ALU.subtract))
            o.wait()
            o(ve.tensor_scalar(lam[:, 5:6], lam[:, 4:5], LAMBDA_INIT, None, ALU.add))
            state_n = [0]
            for n in range(ODD_IN):
                if n == 1:
                    o.wait()
                    o(ve.memset(rstd[:, :], 1.0))
                    o.wait()
                    o(ve.memset(rstd[:, 0:SEQ].rearrange("p (n c) -> p n c", c=CHUNK)[:, :, 0:1], 0.0))
                    o(ve.memset(rstd[:, SEQ:SEQ + 1], 0.0))
                    o(ve.memset(o_st[:, 0], 0.0))
                    ve.wait_ge(side_mm, 5)
                    for j in range(2):
                        gt = gate_tmp[j]
                        o(ve.tensor_scalar(halves(gt[:, 0]), pair(j), const("b_gate")[:, j:j + 1], None, ALU.add))
                        o.wait()
                        o(ve.scalar_tensor_tensor(gt[:, 1], gt[:, 0], -1.0, gt[:, 0], ALU.mult, ALU.max), gate_z)
                if n == 2:
                    for j in range(2):
                        gt = gate_tmp[j]
                        ve.wait_ge(gate_l, j + 1)
                        o(ve.scalar_tensor_tensor(gt[:, 0], gt[:, 0], 0.0, gt[:, 1], ALU.min, ALU.subtract))
                        o.wait()
                        o(ve.tensor_tensor_scan(gt[:, 2], rstd[:, :], gt[:, 0], 0.0, ALU.mult, ALU.add))
                        o.wait()
                        for c0, nc_, w in ((0, SEQ // CHUNK, CHUNK), (SEQ, 1, SMP)):
                            cum = gt[:, 2, c0:c0 + nc_ * w].rearrange("p (n c) -> p n c", c=w)
                            last = cum[:, :, w - 1:w].broadcast_to([P, nc_, w])
                            ins = ve.tensor_tensor(gt[:, 1, c0:c0 + nc_ * w].rearrange("p (n c) -> p n c", c=w),
                                                   last, cum, ALU.subtract)
                            o(ins, cum_ready if c0 else None)
                if n == 4:
                    ve.wait_ge(evac, EVEN_IN + 5)
                    for j in range(2):
                        gt = gate_tmp[j]
                        ve.wait_ge(decays, j + 1)
                        o(ve.tensor_copy(elast[:, j, 0:8].unsqueeze(2),
                                         gt[:, 0, 0:SEQ].rearrange("p (n c) -> p n c", c=CHUNK)[:, :, CHUNK - 1:CHUNK]))
                        o(ve.tensor_copy(elast[:, j, 8:9], gt[:, 0, T - 1:T]))
                        o(ve.tensor_tensor(o_q[:, j], o_q[:, j], gt[:, 0], ALU.mult))
                        o(ve.tensor_tensor(o_kd[:, j], o_k[:, j], gt[:, 3], ALU.mult))
                        o.wait()
                        o(ve.tensor_tensor(o_k[:, j], o_k[:, j], gt[:, 1], ALU.mult), gla_in)
                if n >= 17:
                    h = (n - 17) % 4
                    ve.wait_ge(evac, EVEN_IN + n + 1)
                    o.wait()
                    rotate(oz[:, n % 2], o_swap[:, :], o_rope, d_kT[:, h] if n < 21 else None, d_qT[:, h])
                if n >= GLA_SLOT0:
                    k = n - GLA_SLOT0
                    if k % 2 == 0:
                        if k >= 2:
                            t = k // 2 - 1
                            c0, w = TILES[t]
                            ve.wait_ge(hrms_ready, t + 1)
                            o(ve.tensor_tensor(head_t[:, 0:4 * w], head_t[:, 0:4 * w], r_h[:, 0:4 * w], ALU.mult), head_y)
                            ve.wait_ge(y_hi_done, 9 + t + 1)
                            o(ve.tensor_tensor(y_lo[:, 0:4, c0:c0 + w], head_t[:, 0:4 * w].rearrange("p (e q) -> p e q", e=4),
                                               y_hi[:, 0:4, c0:c0 + w].bitcast(F32), ALU.subtract), y_lo_done)
                        t = k // 2
                        if t < 5:
                            c0, w = TILES[t]
                            ve.wait_ge(att_ready, t + 1)
                            o.wait()
                            o(ve.tensor_tensor(att_m[0:w, 0:4 * w].rearrange("k (p j q) -> k p j q", p=2, j=2),
                                               psum[0:w, 0:2, 0:2 * w].rearrange("k p (j q) -> k p j q", j=2),
                                               causal[0:w, 0:w].unsqueeze(1).unsqueeze(1).broadcast_to([w, 2, 2, w]),
                                               ALU.mult), att_out)
                            for cc in range(2 if t < 4 else 1):
                                n_ = 2 * t + cc
                                s_in = o_s_in if t == 4 else o_st[:, n_ % 4]
                                s_out = o_s_out if t == 4 else o_st[:, (n_ + 1) % 4]
                                o.wait()
                                for j in range(2):
                                    cols = slice(j * P, (j + 1) * P)
                                    o(ve.scalar_tensor_tensor(s_out[:, cols], s_in[:, cols], elast[:, j, n_:n_ + 1],
                                                              psum[:, cc, 256 + j * P:256 + (j + 1) * P],
                                                              ALU.mult, ALU.add), st_ready if j else None)
                    else:
                        t = (k - 1) // 2
                        c0, w = TILES[t]
                        ve.wait_ge(og_ready, t + 1)
                        ve.wait_ge(evac, EVEN_IN + 17)
                        ve.wait_ge(hsq_ready, t + 1)
                        for p in range(2):
                            o(ve.scalar_tensor_tensor(
                                head_t[:, 2 * w * p:2 * w * (p + 1)].rearrange("p (j q) -> p j q", j=2),
                                psum[:, 2 + p, 0:2 * w].rearrange("p (j q) -> p j q", j=2), const("gla_norm"),
                                o_sg[:, 2 * p:2 * p + 2, c0:c0 + w], ALU.mult, ALU.mult), og_read if p else None)

            def odd_max(u):
                b, h = OU[u]
                (_, nq), (_, nk), _ = odd_block(b)
                sm = small[0:nq, u % 2]
                ve.wait_ge(s_ready, 10 + u + 1)
                o(ve.tensor_reduce(sm[:, 0:2], psum[0:nq, 2 * (u % 2):2 * (u % 2) + 2, 0:nk], AX.X, ALU.max))
                o.wait()
                o(ve.tensor_scalar(sm[:, 4:6], sm[:, 0:2], -0.125, None, ALU.mult), negm)

            def odd_normalise(u):
                b, h = OU[u]
                (_, nq), (_, nk), _ = odd_block(b)
                sm = small[0:nq, u % 2]
                ve.wait_ge(e_ready, 10 + u + 1)
                o(ve.reciprocal(sm[:, 20:22], sm[:, 8:10]))
                o.wait()
                o(ve.tensor_tensor(sm[:, 22:23], sm[:, 21:22], lam[0:nq, 5:6], ALU.mult))
                o.wait()
                p0, p1 = probs[u % 2][0:nq, 0:nk], probs[u % 2][0:nq, 512:512 + nk]
                o(ve.tensor_scalar(p1, p1, sm[:, 22:23], None, ALU.mult))
                o.wait()
                o(ve.scalar_tensor_tensor(p0, p0, sm[:, 20:21], p1, ALU.mult, ALU.subtract), p_norm)

            def odd_heads(b):
                (_, nq), _, _ = odd_block(b)
                ve.wait_ge(hrms_ready, 5 + b + 1)
                o(ve.scalar_tensor_tensor(head_t[:, 0:4 * nq], psum[:, 4, 0:4 * nq], dnorm[:, :], r_h[:, 0:4 * nq],
                                          ALU.mult, ALU.mult), head_y)
                ve.wait_ge(y_hi_done, 14 + b + 1)
                low(b, head_t[:, 0:4 * nq].rearrange("p (h q) -> p h q", h=4))

            odd_max(0)
            for u, (b, h) in enumerate(OU):
                if u + 1 < len(OU):
                    odd_max(u + 1)
                odd_normalise(u)
                if h == 0 and b >= 1:
                    odd_heads(b - 1)
                if u % 2 == 1 and u // 2 < KC:
                    out_first(S_ODD_OUT, u // 2, KC, 0)
            odd_heads(4)
            ve.wait_ge(head_sum, 10)
            o(ve.memset(sumsq[:, :], 0.0))
            o.wait()
            for m in range(KC):
                add_out(slab_done if m % 2 else mid_done, (S_ODD_OUT + 4 if m % 2 else KC + 4) + m // 2 + 1, 2 + m % 2, m)
                ve.wait_ge(sum_add, 3 * KC + m)
                add_square(m, 3)
            norm(3)
            ve.wait_ge(out_done, 16 * 14)
            ffn(1, 3, X_ODD + 2 * KC)

            ve.wait_ge(rms_ready, 5)
            o(ve.reciprocal(rstd[:, :], rstd[:, :]))
            o.wait()
            for c in range(KC):
                ve.scalar_tensor_tensor(x[:, c], x[:, c], norm_w[:, 4, c:c + 1], rstd[:, :],
                                        ALU.mult, ALU.mult).then_inc(y_out, 1)


_INS = {"x": (P, KC, T), "weights": (NSLAB, P, 1024), "consts": (P, NCONST), "pool_w": (P, 4, P),
        "swa_v": (P, P), "rope": (P, 2, T), "swa_k": (P, P), "pool_past": (P, 4, PS), "gate_w": (16, 256),
        "lambda": (P, 256), "state": (P, 256), "diff_k": (P, 4, P), "diff_v": (P, 512)}
_OUTS = {"y": (P, KC * T), "pool_new": (P, 4, 2, PS), "swa_v_new": (2, P, P), "swa_k_new": (P, 2, P),
         "state_new": (P, 2, 256), "diff_k_new": (P, 4, T), "diff_v_new": (T, 512), "tails": (P, 2, FC, 4)}


def lay_out(i):
    f = {k: np.asarray(v) for k, v in i.items()}
    out = {}
    tok = np.concatenate([f["x_prompt"][0], f["x_sample"][0]])
    out["x"] = np.ascontiguousarray(tok.T.reshape(KC, P, T).transpose(1, 0, 2))

    w = np.zeros((NSLAB, P, KC, P), np.float32)

    def columns(m):
        return m.reshape(m.shape[0] // P, P, m.shape[1] // P, P).transpose(2, 1, 0, 3)

    e = f["even_w_in"][0]
    q = e[:, 512:1024].reshape(D, 2, 4, 64).transpose(0, 2, 1, 3).reshape(D, 512)
    w[0:EVEN_IN] = columns(np.concatenate([e[:, 0:512], e[:, 1152:1280], e[:, 1024:1152], q], 1))

    def out_slabs(m, s):
        for half in range(2):
            t = m[512 * half:512 * (half + 1)].reshape(4, P, 4, 2, P)
            w[s + 4 * half:s + 4 * half + 4] = t.transpose(2, 1, 3, 0, 4).reshape(4, P, KC, P)

    eo = f["even_w_out"][0]
    eo = np.concatenate([eo[0:512], eo[512:].reshape(2, 4, 64, D).transpose(1, 0, 2, 3).reshape(512, D)])
    out_slabs(eo, S_EVEN_OUT)
    oi = f["odd_w_in"][0]
    swap = [0, 2, 1, 3]
    heads = lambda m: m.reshape(D, 4, P)[:, swap].reshape(D, 512)
    cr = np.zeros((D, P), np.float32)
    cr[:, 0:16] = oi[:, 1536:1552]
    w[S_ODD_IN:S_ODD_OUT] = columns(np.concatenate(
        [cr, oi[:, 0:512], heads(oi[:, 512:1024]), oi[:, 2576:3088], heads(oi[:, 1024:1536]),
         oi[:, 2064:2576], oi[:, 1552:2064]], 1))
    oo = f["odd_w_out"][0]
    out_slabs(np.concatenate([oo[0:512].reshape(4, P, D)[swap].reshape(512, D), oo[512:]]), S_ODD_OUT)
    for n in range(2):
        up = columns(f["ffn_w_up"][n])
        w[S_UP[n]:S_UP[n] + UP:2] = up[0:FC]
        w[S_UP[n] + 1:S_UP[n] + UP:2] = up[FC:]
        down = columns(f["ffn_w_down"][n])
        for part in range(DOWN_PARTS):
            k = min(8, FC - 8 * part)
            w[S_DOWN[n] + part:S_DOWN[n] + DOWN:DOWN_PARTS, :, 0:k] = down[:, :, 8 * part:8 * part + k]
    out["weights"] = w.reshape(NSLAB, P, 1024)

    c = np.zeros((P, NCONST), np.float32)

    def put(name, v):
        c[:, COLS[name][0]:COLS[name][1]] = v

    def chunked(v):
        return v.reshape(-1, P).T

    put("ident", np.eye(P))
    put("ones", 1.0)
    r = np.arange(P)
    put("causal", (r[:, None] <= r[None]) & (r[:, None] // CHUNK == r[None] // CHUNK))
    norms = [f["norm_mix_w"][0], f["norm_ffn_w"][0], f["norm_mix_w"][1], f["norm_ffn_w"][1], f["final_norm_w"]]
    put("norm", chunked(np.stack(norms)))
    put("conv_w", f["ffn_conv_w"].reshape(2, 3, FC, P).transpose(3, 0, 2, 1).reshape(P, -1))
    put("conv_b", chunked(f["ffn_conv_b"]))
    put("conv_past", f["cache_ffn_conv"][:, 0].reshape(2, 2, FC, P).transpose(3, 0, 2, 1).reshape(P, -1))
    put("pool_scale", chunked(f["pool_scale"][0]))
    put("sinks", np.broadcast_to(f["swa_sinks"][0], (P, 8)))
    put("b_gate", chunked(f["gla_b_gate"][0]))
    put("gla_norm", chunked(f["gla_norm_w"][0]))
    put("diff_norm", chunked(f["diff_norm_w"][0]))
    put("eps", EPS)
    put("inv_count", np.concatenate([1.0 / np.minimum(g, np.arange(16) + 1) for g in POOL_W]))
    out["consts"] = c

    out["pool_w"] = np.ascontiguousarray(f["pool_w"][0].transpose(1, 0, 2))
    out["swa_v"] = f["cache_swa_v"][0, 0].reshape(PAST, P)
    out["swa_k"] = np.ascontiguousarray(f["cache_swa_k"][0, 0].reshape(PAST, P).T)
    out["pool_past"] = np.ascontiguousarray(f["cache_pool"][0, 0].T.reshape(4, P, PS).transpose(1, 0, 2))
    pos = np.concatenate([np.arange(SEQ), PAST + np.arange(SMP)]).astype(np.float32)
    half = ROT // 2
    inv = np.exp(np.float32(-math.log(THETA)) * np.arange(half, dtype=np.float32) * np.float32(2.0 / ROT))
    ang = (pos[None] * inv.astype(np.float32)[:, None]).astype(np.float32)
    rope = np.zeros((2, 64, 2, T), np.float32)
    rope[:, :, 0] = 1.0
    rope[:, 0:half, 0] = rope[:, half:ROT, 0] = np.cos(ang)
    rope[:, 0:half, 1] = -np.sin(ang)
    rope[:, half:ROT, 1] = np.sin(ang)
    out["rope"] = rope.reshape(P, 2, T)
    out["gate_w"] = f["gla_w_gate2"][0]
    out["lambda"] = np.ascontiguousarray(np.broadcast_to(f["diff_lambda"][0].reshape(1, 256), (P, 256)))
    out["state"] = np.ascontiguousarray(f["state_gla"][0, 0].reshape(2, P, P).transpose(1, 0, 2)).reshape(P, 256)
    out["diff_k"] = np.ascontiguousarray(f["cache_diff_k"][0, 0].reshape(PAST, 4, P).transpose(2, 1, 0))
    out["diff_v"] = f["cache_diff_v"][0, 0].reshape(PAST, 512)
    return out


def take_out(r):
    y = r["y"].reshape(P, KC, T).transpose(2, 1, 0).reshape(T, D)
    pool = r["pool_new"].transpose(2, 3, 1, 0).reshape(2, 1, 1, PS, 512)
    k = r["swa_k_new"].transpose(1, 2, 0).reshape(2, 1, 1, P, 2, 64)
    v = r["swa_v_new"].reshape(2, 1, 1, P, 2, 64)
    st = r["state_new"].reshape(P, 2, 2, P).transpose(1, 2, 0, 3).reshape(2, 1, 1, 4, 64, P)
    dk = r["diff_k_new"].transpose(2, 1, 0).reshape(T, 4, 2, 64)
    dv = r["diff_v_new"].reshape(T, 4, P)
    ffn = r["tails"].reshape(P, 2, FC, 2, 2).transpose(3, 1, 4, 2, 0).reshape(2, 2, 1, 2, FF)

    def g(n):
        s = slice(0, SEQ) if n == 0 else slice(SEQ, T)
        return (pool[n], k[n], v[n], st[n], dk[s][None, None], dv[s][None, None], ffn[n])

    return tuple(np.ascontiguousarray(a) for a in (y[None, 0:SEQ], y[None, SEQ:T], *g(0), *g(1)))


def kernel(**inputs):
    import concourse.bacc as bacc
    from concourse.bass_utils import run_bass_kernel_spmd

    nc = bacc.Bacc("TRN2", target_bir_lowering=False, num_devices=1)
    arrays = lay_out(inputs)
    io = {n: nc.dram_tensor(f"in_{n}", s, F32, kind="ExternalInput").ap() for n, s in _INS.items()}
    io |= {n: nc.dram_tensor(f"out_{n}", s, F32, kind="ExternalOutput").ap() for n, s in _OUTS.items()}
    build(nc, io)
    r = run_bass_kernel_spmd(nc, [{f"in_{n}": arrays[n] for n in _INS}], core_ids=[0])
    return take_out({n: r.results[0][f"out_{n}"] for n in _OUTS})
```

```python
import math
from contextlib import ExitStack

import concourse.bass as bass
import numpy as np
from concourse import mybir

F32 = mybir.dt.float32
F32R = mybir.dt.float32r
BF16 = mybir.dt.bfloat16
ALU = mybir.AluOpType
ACT = mybir.ActivationFunctionType
AX = mybir.AxisListType

P = 128
D, SEQ, SMP, PAST = 1024, 512, 32, 128
T = SEQ + SMP
HALF = T // 2
KC = D // P
FF = 2816
FC = FF // P
CHUNK = 64
EPS = 1e-6
NEG = -1e30
LAMBDA_INIT = 0.8 - 0.6 * math.exp(-0.3 * 1)
POOL_W = (2, 4, 8, 16)
PS = 15
UE = PS + SEQ + PS + SMP
GE = 2 + SEQ + 2 + SMP
CO = SEQ + 2 + SMP
KEYS = SEQ + PAST + SMP
THETA, ROT = 500000.0, 16

EVEN_IN, ODD_IN, OUT, UP, DOWN_PARTS = 10, 25, 8, 2 * FC, 3
DOWN = KC * DOWN_PARTS
S_EVEN_OUT = EVEN_IN
S_UP = [EVEN_IN + OUT, 0]
S_DOWN = [S_UP[0] + UP, 0]
S_ODD_IN = S_DOWN[0] + DOWN
S_ODD_OUT = S_ODD_IN + ODD_IN
S_UP[1] = S_ODD_OUT + OUT
S_DOWN[1] = S_UP[1] + UP
NSLAB = S_DOWN[1] + DOWN
RING, RAW = 4, 2

COLS = {}
_at = 0
for _name, _n in (("ident", 128), ("ones", 128), ("causal", 128), ("norm", 5 * KC), ("conv_w", 2 * FC * 3),
                  ("conv_b", 2 * FC), ("conv_past", 2 * FC * 2), ("pool_scale", 4), ("sinks", 8),
                  ("b_gate", 2), ("gla_norm", 1), ("diff_norm", 1), ("eps", 1), ("inv_count", 64)):
    COLS[_name] = (_at, _at + _n)
    _at += _n
NCONST = _at

ODD_CHUNKS = (["cr"] + ["cq"] * 2 + ["ck"] * 2 + ["cv"] * 4 + ["dv"] * 4 + ["cg"] * 4 + ["dk"] * 4 + ["dq"] * 4)
EVEN_CHUNKS = ["u"] * 4 + ["v", "k"] + ["q"] * 4
V_KW0, V_ALL = 9, 11
T_STATES = [2, 4, 6, 8, 9]
X_ODD = 3 * KC
NEVEN, NODD, NOUT = 5, 4, 23
PARTNER = [(k + 8) % 16 if k < 16 else k for k in range(32)]
GLA_SLOT0 = 14
TILES = [(t * P, P if t < 4 else SMP) for t in range(5)]


def build(nc, io):
    ctx = ExitStack()
    with ctx:
        base = 16512
        top = [base]

        def at(name, shape, dt, offset):
            return nc.alloc_sbuf_tensor_at(name, shape, dt, offset=offset)

        def sb(name, shape, dt=F32):
            size = int(np.prod(shape[1:])) * (2 if dt == BF16 else 4)
            size = (size + 31) // 32 * 32
            t = at(name, shape, dt, top[0])
            top[0] += size
            return t

        x = sb("x", [P, KC, T])
        h_at = top[0]
        h_hi = sb("h_hi", [P, KC, T], F32R)
        h_lo_at = top[0]
        h_lo = sb("h_lo", [P, KC, T], F32R)
        y_at = top[0]
        y_hi = sb("y_hi", [P, FC, T], F32R)
        y_lo_at = top[0]
        y_lo = sb("y_lo", [P, FC, T], F32R)
        w_hi = sb("w_hi", [P, RING, 1024], F32R)
        w_lo = sb("w_lo", [P, RING, 1024], F32R)
        w_raw = sb("w_raw", [P, RAW, 1024])
        sumsq = sb("sumsq", [P, T])
        rstd = sb("rstd", [P, T])
        sq_at = top[0]
        sq = sb("sq", [P, 2, T])
        ffn_at = top[0]
        gate = [sb(f"gate{p}", [P, GE]) for p in range(2)]
        conv = [sb(f"conv{p}", [P, CO]) for p in range(2)]
        consts = sb("consts", [P, NCONST])
        tails = sb("tails", [P, FC, 4])
        mask_q = sb("mask_q", [P, 2, P], BF16)
        mask_k = sb("mask_k", [P, CHUNK], BF16)
        small = sb("small", [P, 2, 24])
        elast = sb("elast", [P, 2, 9])
        lam = sb("lam", [P, 8])
        tick = sb("tick", [1, 1])
        dnorm = sb("dnorm", [P, 1])
        assert top[0] <= nc.sbuf_usable_end, (top[0], nc.sbuf_usable_end)

        def const(name, *shape):
            a, b = COLS[name]
            v = consts[:, a:b]
            if len(shape) == 2:
                v = v.rearrange("p (a b) -> p a b", a=shape[0])
            if len(shape) == 3:
                v = v.rearrange("p (a b c) -> p a b c", a=shape[0], b=shape[1])
            return v

        ident, ones, causal = const("ident"), const("ones"), const("causal")
        norm_w = const("norm", 5, KC)
        conv_w, conv_b, conv_past = const("conv_w", 2, FC, 3), const("conv_b", 2, FC), const("conv_past", 2, FC, 2)
        eps = const("eps")

        def region(prefix, start, end):
            here = [start]

            def take(name, shape):
                t = at(prefix + name, shape, F32, here[0])
                here[0] += (int(np.prod(shape[1:])) * 4 + 31) // 32 * 32
                assert here[0] <= end, name
                return t
            return take

        r1 = region("even_", y_at + 4 * T * 4, y_lo_at)
        r2 = region("even_", y_lo_at + 4 * T * 4, y_lo_at + FC * T * 4)
        ez = r1("z", [P, 2, T])
        e_vT = r1("vT", [P, T])
        e_v = r1("v", [P, 5, P])
        e_kT = r1("kT", [P, KEYS])
        e_qT = r1("qT", [P, 4, T])
        e_u = r1("u", [P, 4, UE])
        e_wpool = r1("wpool", [P, 4, P])
        e_vc = r1("vc", [P, P])
        e_rope = r1("rope", [P, 2, T])
        e_w = r2("winsum", [P, 2, UE])
        e_diff = r2("diff", [P, 4, T])
        e_swap = r2("rope_swapped", [P, T])

        r1 = region("odd_", y_at + 4 * T * 4, y_lo_at)
        r2 = region("odd_", y_lo_at + 4 * T * 4, y_lo_at + FC * T * 4)
        oz = r1("z", [P, 2, T])
        o_cr = r1("cr", [P, T])
        o_swap = at("odd_rope_swapped", [P, T], F32, y_at + 4 * T * 4 + 2 * T * 4)
        o_wg = r1("wgate_then_state", [P, 256])
        o_q = r1("gla_q", [P, 2, T])
        o_k = r1("gla_k", [P, 2, T])
        o_kd = r1("gla_kd", [P, 2, T])
        o_sg = r1("silu", [P, 4, T])
        o_rope = r1("rope", [P, 2, T])
        o_st = r1("states", [P, 4, 256])
        o_lp = r1("lambda_in", [P, 256])
        o_cv = r2("cv", [P, 5, 512])
        o_dv = r2("dv", [P, 5, 512])
        o_kw = r2("kw", [P, 5, 256])
        dk_at = y_lo_at + 4 * T * 4 + (2 * 2560 + 1280) * 4
        d_kT = r2("kT", [P, 4, KEYS])
        d_vc = r2("vc", [P, 512])
        gate_tmp = [at("gate_tmp0", [P, 4, T], F32, dk_at), at("gate_tmp1", [P, 4, T], F32, ffn_at)]
        d_qT = at("d_qT", [P, 4, T], F32, ffn_at)
        probs = [at(f"probs{b}", [P, 1024], F32, h_at + b * 4096) for b in range(2)]
        probsT = [at(f"probsT{b}", [P, 2, 512], F32, h_lo_at + b * 4096) for b in range(2)]
        att_m = at("att_masked", [P, 512], F32, sq_at)
        head_t = at("head_tmp", [P, 512], F32, sq_at + 2048)
        sq_h = sumsq[:, 0:512]
        r_h = at("head_rstd", [P, 512], F32, y_at + 4 * T * 4 + 3 * T * 4 + 1024 + 2 * T * 4)
        resets = sq[:, 0]
        o_s_in = sb("sample_state", [P, 256])
        o_s_out = o_wg

        psum = ctx.enter_context(nc.psum_tensor("psum", [P, 8, 512], F32))

        def pair(k):
            return psum[:, 2 * k:2 * k + 2, 0:HALF]

        def pieces(k):
            return [(psum[:, 2 * k, 0:HALF], 0, HALF),
                    (psum[:, 2 * k + 1, 0:SEQ - HALF], HALF, SEQ - HALF),
                    (psum[:, 2 * k + 1, SEQ - HALF:HALF], SEQ, SMP)]

        def halves(v):
            return v.rearrange("p (h t) -> p h t", h=2)

        def sem(name):
            return ctx.enter_context(nc.semaphore(name))

        in_x = [sem(f"in_x{c}") for c in range(KC)]
        in_const = sem("in_const")
        in_even, in_odd = sem("in_even"), sem("in_odd")
        in_w = [sem(f"in_w{r}") for r in range(RAW)]
        out_done = sem("out_done")
        ticks = sem("ticks")
        w_hi_done, w_ready = sem("w_hi_done"), sem("w_ready")
        slab_done, mid_done = sem("slab_done"), sem("mid_done")
        sum_ready = sem("sum_ready")
        turned, side_mm = sem("turned"), sem("side_mm")
        s_ready, p_turned, o_ready = sem("s_ready"), sem("p_turned"), sem("o_ready")
        att_ready, og_ready = sem("att_ready"), sem("og_ready")
        head_sum = sem("head_sum")
        act, vec = sem("act"), sem("vec")
        sq_ready, rms_ready, h_hi_done = sem("sq_ready"), sem("rms_ready"), sem("h_hi_done")
        evac = sem("evac")
        silu_in = sem("silu_in")
        v_out = sem("v_out")
        e_ready, pT_out, y_hi_done = sem("e_ready"), sem("pT_out"), sem("y_hi_done")
        gate_l, decays = sem("gate_l"), sem("decays")
        gelu_ready, ffn_hi = sem("gelu_ready"), sem("ffn_hi")
        gate_out, val_out = sem("gate_out"), sem("val_out")
        hsq_ready, hrms_ready = sem("hsq_ready"), sem("hrms_ready")
        setup = sem("setup")
        sum_add, h_ready = sem("sum_add"), sem("h_ready")
        x_upd = sem("x_upd")
        rope_done, diff_ready = sem("rope_done"), sem("diff_ready")
        y_lo_done = sem("y_lo_done")
        negm, p_norm = sem("negm"), sem("p_norm")
        gate_z, cum_ready, gla_in = sem("gate_z"), sem("cum_ready"), sem("gla_in")
        att_out, st_ready = sem("att_out"), sem("st_ready")
        head_out = sem("head_out")
        og_read, head_y = sem("og_read"), sem("head_y")
        conv_ready, y_f, y_ready = sem("conv_ready"), sem("y_f"), sem("y_ready")
        lam_sum, lam_exp = sem("lam_sum"), sem("lam_exp")
        in_cache = sem("in_cache")
        y_out = sem("y_out")

        EU = [(b, g) for b in range(5) for g in range(2)]
        OU = [(b, h) for b in range(5) for h in range(4)]

        def even_block(b):
            if b == 4:
                return (SEQ, SMP), (SEQ, PAST + SMP), [("cache", P), (4, SMP)]
            lo = max(b - 1, 0)
            return (b * P, P), (lo * P, (b + 1 - lo) * P), [(t, P) for t in range(lo, b + 1)]

        def odd_block(b):
            if b == 4:
                return (SEQ, SMP), (SEQ, PAST + SMP), [("cache", P), (4, SMP)]
            return (b * P, P), (0, (b + 1) * P), [(t, P) for t in range(b + 1)]

        def s_even(u):
            b = u % 2
            return psum[:, 2 * b:2 * b + 2, :].rearrange("p c (h k) -> p (c h) k", h=2)

        class Order:

            def __init__(self, eng, own):
                self.eng, self.own, self.n = eng, own, {}
                self.last = None

            def __call__(self, ins, sem_=None):
                s = self.own if sem_ is None else sem_
                ins.then_inc(s, 1)
                self.n[s.name] = self.n.get(s.name, 0) + 1
                self.last = (s, self.n[s.name])
                return self.n[s.name]

            def wait(self):
                self.eng.wait_ge(*self.last)

        def settle(eng):
            eng.wait_ge(in_const, 16)

        block = ctx.enter_context(nc.Block())

        @block.sync
        def _(sp):
            def load(s, r):
                sp.dma_start(w_raw[:, r], io["weights"][s]).then_inc(in_w[r], 16)

            for s in range(RAW):
                load(s, s)
            for s in range(RAW, RING):
                sp.wait_ge(w_ready, s - RAW + 1)
                load(s, s % RAW)
            with sp.Fori(1, NSLAB // RING) as i:
                for k in range(RING):
                    sp.wait_ge(w_ready, RING * i + (k - RAW + 1))
                    load(RING * i + k, k % RAW)
            for s in range(NSLAB // RING * RING, NSLAB):
                sp.wait_ge(w_ready, s - RAW + 1)
                load(s, s % RAW)
            for c in range(KC):
                sp.wait_ge(y_out, c + 1)
                sp.dma_start(io["y"][:, c * T:(c + 1) * T], x[:, c]).then_inc(out_done, 16)
            sp.wait_ge(out_done, 16 * NOUT)

        @block.gpsimd
        def _(pool):
            pool.memset(tick[:, :], 0.0).then_inc(ticks, 1)

            def split(i, k, first=False):
                s = RING * i + k
                pool.wait_ge(in_w[k % RAW], (RING // RAW) * 16 * i + 16 * (k // RAW + 1))
                if not first:
                    pool.wait_ge(ticks, 1)
                    pool.wait_ge(slab_done, s - RING + 1)
                    pool.tensor_tensor(tick[:, :], tick[:, :], tick[:, :], ALU.mult).then_inc(ticks, 1)
                pool.tensor_scalar(w_hi[:, k], w_raw[:, k % RAW], 1.0, 0.0, ALU.mult, ALU.add).then_inc(w_hi_done, 1)
                pool.wait_ge(w_hi_done, s + 1)
                pool.tensor_tensor(w_lo[:, k], w_raw[:, k % RAW], w_hi[:, k].bitcast(F32),
                                   ALU.subtract).then_inc(w_ready, 1)

            for k in range(RING):
                split(0, k, first=True)
            with pool.Fori(1, NSLAB // RING) as i:
                for k in range(RING):
                    split(i, k)
            for s in range(NSLAB // RING * RING, NSLAB):
                split(s // RING, s % RING)

        @block.tensor
        def _(pe):
            def tiles(acc, s, pairs, first, last):
                for n, (kt, xh, xl) in enumerate(pairs):
                    wh = w_hi[:, s % RING, kt * P:(kt + 1) * P]
                    wl = w_lo[:, s % RING, kt * P:(kt + 1) * P]
                    for half in range(2):
                        cols = slice(half * HALF, (half + 1) * HALF)
                        out = psum[:, 2 * acc + half, 0:HALF]
                        pe.matmul(out, wh, xh[:, cols], start=first and n == 0, stop=False)
                        pe.matmul(out, wh, xl[:, cols], start=False, stop=False)
                        ins = pe.matmul(out, wl, xh[:, cols], start=False, stop=last and n == len(pairs) - 1)
                return ins

            def h_tiles(c0, c1):
                return [(c, h_hi[:, c], h_lo[:, c]) for c in range(c0, c1)]

            def total(n, acc):
                pe.wait_ge(sum_add, KC * (n + 1))
                for half in range(2):
                    ins = pe.matmul(psum[:, 2 * acc + half, 0:HALF], ones, sumsq[:, half * HALF:(half + 1) * HALF],
                                    start=True, stop=True)
                ins.then_inc(sum_ready, 1)

            def in_projection(n_norm, s0, ev0, chunks, side):
                for n in range(chunks):
                    pe.wait_ge(w_ready, s0 + n + 1)
                    if n >= 2:
                        pe.wait_ge(evac, ev0 + n - 1)
                    for c in range(KC):
                        if n == 0:
                            pe.wait_ge(h_ready, KC * n_norm + c + 1)
                        ins = tiles(2 + n % 2, s0 + n, h_tiles(c, c + 1), c == 0, c == KC - 1)
                    ins.then_inc(slab_done, 1)
                    if n == 0:
                        total(n_norm, 0)
                    side(n)

            def out_chunk(s, m, acc, yh, yl, c0):
                pe.wait_ge(w_ready, s + 1)
                part = [(4 * (m % 2) + c, yh[:, c0 + c], yl[:, c0 + c]) for c in range(4)]
                tiles(acc, s, part, True, True).then_inc(slab_done if m % 2 else mid_done, 1)

            def ffn(layer, n_norm, upd0):
                s0, d0, f0 = S_UP[layer], S_DOWN[layer], FC * layer

                def up(i, k, fresh=False):
                    pe.wait_ge(w_ready, RING * i + (s0 + k + 1))
                    if not fresh:
                        pe.wait_ge(val_out if k % 2 else gate_out, 2 * i + (f0 + k // 2 - 1))
                    tiles(k, s0 + k, h_tiles(0, KC), True, True).then_inc(slab_done, 1)

                pe.wait_ge(w_ready, s0 + 2)
                for c in range(KC):
                    pe.wait_ge(h_ready, KC * n_norm + c + 1)
                    for k in range(2):
                        ins = tiles(k, s0 + k, h_tiles(c, c + 1), c == 0, c == KC - 1)
                        if c == KC - 1:
                            ins.then_inc(slab_done, 1)
                total(n_norm, 3)
                up(0, 2, fresh=True)
                pe.wait_ge(rms_ready, n_norm + 1)
                up(0, 3, fresh=True)
                with pe.Fori(1, FC // 2) as i:
                    for k in range(RING):
                        up(i, k)

                def down(i, j):
                    for part in range(DOWN_PARTS):
                        k = DOWN_PARTS * j + part
                        pe.wait_ge(w_ready, 4 * DOWN_PARTS * i + (d0 + k + 1))
                        lo, hi = 8 * part, min(8 * part + 8, FC)
                        if part == 0:
                            pe.wait_ge(x_upd, 4 * i + (upd0 + j - 1))
                            if j < 2:
                                pe.wait_ge(val_out, f0 + FC - 1)
                        for f in range(lo, hi):
                            if j == 0:
                                pe.wait_ge(y_ready, f0 + f + 1)
                            ins = tiles(j % 2, d0 + k, [(f - lo, y_hi[:, f], y_lo[:, f])], f == 0, f == FC - 1)
                        ins.then_inc(slab_done, 1)

                with pe.Fori(0, 2) as i:
                    for j in range(4):
                        down(i, j)

            pe.wait_ge(in_const, 16)
            pe.wait_ge(setup, 1)

            def even_side(n):
                if n == 5:
                    pe.wait_ge(evac, 5)
                    pe.wait_ge(rms_ready, 1)
                    for t, (c, w) in enumerate(TILES):
                        ins = pe.transpose(psum[0:w, t // 4, (t % 4) * P:(t % 4 + 1) * P], e_vT[:, c:c + w], ident)
                    ins.then_inc(turned, 1)
                if n >= 6:
                    g = n - 6
                    if g == 0:
                        pe.wait_ge(in_even, 16 * NEVEN)
                    pe.wait_ge(diff_ready, g + 1)
                    if g == 1:
                        pe.wait_ge(v_out, 1)
                    if g >= 2:
                        pe.wait_ge(y_lo_done, g - 1)
                    acc = (g + 1) % 2
                    for half in range(2):
                        ins = pe.matmul(psum[:, 2 * acc + half, 0:HALF], e_wpool[:, g],
                                        e_diff[:, g, half * HALF:(half + 1) * HALF], start=True, stop=True)
                    ins.then_inc(side_mm, 1)

            in_projection(0, 0, 0, EVEN_IN, even_side)

            def even_scores(u):
                b, g = EU[u]
                (q0, nq), (k0, nk), _ = even_block(b)
                if u < 2:
                    pe.wait_ge(rope_done, 5)
                    pe.wait_ge(y_lo_done, 4)
                else:
                    pe.wait_ge(pT_out, u - 1)
                rows = slice(64 * g, 64 * g + 64)
                S = s_even(u)
                for j in range(4):
                    ins = pe.matmul(S[0:nq, j, 0:nk], e_qT[rows, j, q0:q0 + nq], e_kT[rows, k0:k0 + nk],
                                    start=True, stop=b == 4)
                    if b < 4:
                        ins = pe.matmul(S[0:nq, j, nk - CHUNK:nk], mask_q[rows, 0], mask_k[rows],
                                        start=False, stop=b == 0)
                    if 0 < b < 4:
                        ins = pe.matmul(S[0:nq, j, 0:CHUNK], mask_q[rows, 1], mask_k[rows], start=False, stop=True)
                ins.then_inc(s_ready, 1)

            even_scores(0)
            even_scores(1)
            for u, (b, g) in enumerate(EU):
                (q0, nq), _, runs = even_block(b)
                pe.wait_ge(p_norm, u + 1)
                pr = probs[u % 2][:, :].rearrange("p (h k) -> p h k", h=4)
                for kb, (_, kn) in enumerate(runs):
                    for j in range(4):
                        ins = pe.transpose(psum[0:kn, 2 * (u % 2) + kb, j * nq:(j + 1) * nq],
                                           pr[0:nq, j, kb * P:kb * P + kn], ident[0:nq, 0:nq])
                ins.then_inc(p_turned, 1)
                if u < KC:
                    if u >= 1:
                        pe.wait_ge(x_upd, u)
                    else:
                        pe.wait_ge(evac, EVEN_IN)
                    out_chunk(S_EVEN_OUT + u // 2, u, 3, y_hi, y_lo, 0)
                pe.wait_ge(pT_out, u + 1)
                if g == 0 and b >= 2:
                    pe.wait_ge(y_lo_done, 4 + b - 1)
                for kb, (t, kn) in enumerate(runs):
                    v = e_vc[0:kn, 64 * g:64 * g + 64] if t == "cache" else e_v[0:kn, t, 64 * g:64 * g + 64]
                    ins = pe.matmul(psum[64 * g:64 * g + 64, 4 + b % 2, 0:4 * nq], v, probsT[u % 2][0:kn, kb, 0:4 * nq],
                                    start=kb == 0, stop=kb == len(runs) - 1)
                ins.then_inc(o_ready, 1)
                if u + 2 < len(EU):
                    even_scores(u + 2)
            pe.wait_ge(y_lo_done, 9)
            for m in range(KC):
                pe.wait_ge(x_upd, KC + m - 1)
                out_chunk(S_EVEN_OUT + 4 + m // 2, m, 2 + m % 2, h_hi, h_lo, 4)
            ffn(0, 1, 2 * KC)

            def turn(n, src, waits):
                for s, v in waits:
                    pe.wait_ge(s, v)
                for t, (c, w) in enumerate(TILES):
                    ins = pe.transpose(psum[0:w, t // 4, (t % 4) * P:(t % 4 + 1) * P], src[:, c:c + w], ident)
                ins.then_inc(turned, 1)

            def odd_side(n):
                if n == 1:
                    pe.wait_ge(in_odd, 16 * NODD)
                    pe.wait_ge(evac, EVEN_IN + 1)
                    for j in range(2):
                        for half in range(2):
                            ins = pe.matmul(psum[:, 2 * j + half, 0:HALF], o_wg[0:16, j * P:(j + 1) * P],
                                            o_cr[0:16, half * HALF:(half + 1) * HALF], start=True, stop=True)
                    ins.then_inc(side_mm, 1)
                if 6 <= n < 14:
                    waits = [(evac, EVEN_IN + n)]
                    waits += [(v_out, 1 + n - 6)] if n > 6 else [(gate_z, 2)]
                    turn(n, oz[:, (n - 1) % 2], waits)
                if n == 12:
                    pe.wait_ge(gla_in, 2)
                    for t in range(4):
                        for j in range(2):
                            ins = pe.transpose(psum[:, 2 + t // 2, (2 * (t % 2) + j) * P:(2 * (t % 2) + j + 1) * P],
                                               o_k[:, j, t * P:(t + 1) * P], ident)
                    ins.then_inc(side_mm, 1)
                if n == 13:
                    pe.wait_ge(v_out, V_KW0)
                    for j in range(2):
                        ins = pe.transpose(psum[0:SMP, 2, j * P:(j + 1) * P], o_k[:, j, SEQ:T], ident)
                    ins.then_inc(side_mm, 1)
                if n >= GLA_SLOT0:
                    k = n - GLA_SLOT0
                    if k % 2 == 0:
                        if k >= 2:
                            t = k // 2 - 1
                            w = TILES[t][1]
                            pe.wait_ge(hsq_ready, t + 1)
                            pe.wait_ge(og_read, t + 1)
                            for p in range(2):
                                ins = pe.matmul(psum[:, 2 + p, 256:256 + 2 * w], ones, sq_h[:, 2 * w * p:2 * w * (p + 1)],
                                                start=True, stop=True)
                            ins.then_inc(head_sum, 1)
                        if k // 2 < 5:
                            stage_a(k // 2)
                    else:
                        stage_b((k - 1) // 2)

            def stage_a(t):
                c0, w = TILES[t]
                if t == 0:
                    pe.wait_ge(v_out, V_ALL)
                else:
                    pe.wait_ge(st_ready, T_STATES[t - 1])
                for j in range(2):
                    for p in range(2):
                        pe.matmul(psum[0:w, p, j * w:(j + 1) * w], o_kd[64 * p:64 * p + 64, j, c0:c0 + w],
                                  o_q[64 * p:64 * p + 64, j, c0:c0 + w], start=True, stop=True)
                for cc in range(2 if t < 4 else 1):
                    r = slice(64 * cc, 64 * cc + min(w, 64))
                    for j in range(2):
                        for p in range(2):
                            e = 2 * p + j
                            ins = pe.matmul(psum[64 * p:64 * p + 64, cc, 256 + j * P:256 + (j + 1) * P],
                                            o_kw[r, t, j * P + 64 * p:j * P + 64 * p + 64],
                                            o_cv[r, t, e * P:(e + 1) * P], start=True, stop=True)
                ins.then_inc(att_ready, 1)

            def stage_b(t):
                c0, w = TILES[t]
                pe.wait_ge(att_out, t + 1)
                pe.wait_ge(st_ready, T_STATES[t] - (1 if t < 4 else 1))
                if t >= 1:
                    pe.wait_ge(head_y, t)
                for p in range(2):
                    for j in range(2):
                        e = 2 * p + j
                        out = psum[:, 2 + p, j * w:(j + 1) * w]
                        pe.matmul(out, o_cv[0:w, t, e * P:(e + 1) * P], att_m[0:w, e * w:(e + 1) * w],
                                  start=True, stop=False)
                        for cc in range(2 if t < 4 else 1):
                            st = o_s_in if t == 4 else o_st[:, (2 * t + cc) % 4]
                            cw = min(w, CHUNK)
                            ins = pe.matmul(out[:, cc * CHUNK:cc * CHUNK + cw],
                                            st[64 * p:64 * p + 64, j * P:(j + 1) * P],
                                            o_q[64 * p:64 * p + 64, j, c0 + cc * CHUNK:c0 + cc * CHUNK + cw],
                                            start=False, stop=(cc == 1 or t == 4))
                ins.then_inc(og_ready, 1)

            in_projection(2, S_ODD_IN, EVEN_IN, ODD_IN, odd_side)

            def odd_scores(u):
                b, h = OU[u]
                (q0, nq), (k0, nk), _ = odd_block(b)
                if u < 2:
                    pe.wait_ge(rope_done, 5 + 8)
                    pe.wait_ge(y_lo_done, 9 + 5)
                    pe.wait_ge(in_cache, 32)
                else:
                    pe.wait_ge(pT_out, 10 + u - 1)
                for c in range(2):
                    rows = slice(64 * c, 64 * c + 64)
                    S = psum[0:nq, 2 * (u % 2) + c, 0:nk]
                    ins = pe.matmul(S, d_qT[rows, h, q0:q0 + nq], d_kT[rows, h, k0:k0 + nk],
                                    start=True, stop=b == 4)
                    if b < 4:
                        ins = pe.matmul(psum[0:nq, 2 * (u % 2) + c, nk - CHUNK:nk], mask_q[rows, 0], mask_k[rows],
                                        start=False, stop=True)
                ins.then_inc(s_ready, 1)

            odd_scores(0)
            odd_scores(1)
            for u, (b, h) in enumerate(OU):
                (q0, nq), _, runs = odd_block(b)
                pe.wait_ge(p_norm, 10 + u + 1)
                for kb, (_, kn) in enumerate(runs):
                    ins = pe.transpose(psum[0:kn, 2 * (u % 2), kb * nq:(kb + 1) * nq],
                                       probs[u % 2][0:nq, kb * P:kb * P + kn], ident[0:nq, 0:nq])
                ins.then_inc(p_turned, 1)
                if u % 2 == 0 and u // 2 < KC:
                    m = u // 2
                    if m >= 1:
                        pe.wait_ge(x_upd, X_ODD + m)
                    else:
                        pe.wait_ge(evac, EVEN_IN + ODD_IN)
                    out_chunk(S_ODD_OUT + m // 2, m, 3, y_hi, y_lo, 0)
                pe.wait_ge(pT_out, 10 + u + 1)
                if h == 0 and b >= 1:
                    pe.wait_ge(head_out, b)
                for kb, (t, kn) in enumerate(runs):
                    v = d_vc[0:kn, h * P:(h + 1) * P] if t == "cache" else o_dv[0:kn, t, h * P:(h + 1) * P]
                    ins = pe.matmul(psum[:, 4, h * nq:(h + 1) * nq], v, probsT[u % 2][0:kn, 0, kb * nq:(kb + 1) * nq],
                                    start=kb == 0, stop=kb == len(runs) - 1)
                ins.then_inc(o_ready, 1)
                if u + 2 < len(OU):
                    odd_scores(u + 2)
                if h == 3:
                    pe.wait_ge(hsq_ready, 5 + b + 1)
                    pe.matmul(psum[:, 5, 0:4 * nq], ones, sq_h[:, 0:4 * nq], start=True, stop=True)\
                        .then_inc(head_sum, 1)
            pe.wait_ge(y_lo_done, 9 + 10)
            for m in range(KC):
                pe.wait_ge(x_upd, X_ODD + KC + m - 1)
                out_chunk(S_ODD_OUT + 4 + m // 2, m, 2 + m % 2, h_hi, h_lo, 4)
            ffn(1, 3, X_ODD + 2 * KC)
            total(4, 2)

        @block.scalar
        def _(ac):
            o = Order(ac, act)
            loop = [None]

            def square(c, n, i=None):
                if i is not None:
                    settle(ac)
                o(ac.activation(sq[:, c % 2], x[:, c] if i is None else x[:, 4 * i + c], ACT.Square), sq_ready)

            def norm_hi(c, n, i=None):
                ch = c if i is None else 4 * i + c
                if i is not None:
                    settle(ac)
                w = norm_w[:, n, c:c + 1] if i is None else norm_w[:, n, bass.ds(ch, 1)]
                ac.activation(h_hi[:, ch], x[:, ch], ACT.Copy, scale=w).then_inc(h_hi_done, 1)

            def rms(n, acc):
                ac.wait_ge(sum_ready, n + 1)
                o(ac.activation(halves(rstd), pair(acc), ACT.Sqrt, bias=eps, scale=1.0 / D), rms_ready)

            def dma(dst, src, s):
                ac.dma_start(dst, src).then_inc(s, 16)

            def ffn(layer, n_norm, upd0):
                s0, d0, f0, g0 = S_UP[layer], S_DOWN[layer], FC * layer, KC * n_norm

                def chunk(i, p):
                    f = 2 * i + p
                    ac.wait_ge(conv_ready, 2 * i + (f0 + p + 1))
                    settle(ac)
                    ac.activation(conv[p][:, :], conv[p][:, :], ACT.Gelu_apprx_tanh,
                                  bias=conv_b[:, layer, f:f + 1] if isinstance(i, int) else
                                  conv_b[:, layer, bass.ds(f, 1)]).then_inc(gelu_ready, 1)
                    ac.wait_ge(y_f, 2 * i + (f0 + p + 1))
                    settle(ac)
                    ac.activation(y_hi[:, f], sq[:, p], ACT.Copy).then_inc(ffn_hi, 1)

                rms(n_norm, 3)
                with ac.Fori(0, FC // 2) as i:
                    for p in range(2):
                        chunk(i, p)
                with ac.Fori(0, 2) as i:
                    for j in range(4):
                        ac.wait_ge(x_upd, 4 * i + (upd0 + j + 1))
                        ac.wait_ge(sum_add, 4 * i + (g0 + KC + j - 1))
                        if n_norm < 3:
                            norm_hi(j, n_norm + 1, i)
                        square(j, n_norm + 1, i)

            def out_norm(n, upd0):
                for m in range(KC):
                    ac.wait_ge(x_upd, upd0 + m + 1)
                    if m < 4:
                        norm_hi(m, n)
                    ac.wait_ge(sum_add, KC * n + m - 1)
                    square(m, n)
                for m in range(4, KC):
                    norm_hi(m, n)

            dma(consts[:, :], io["consts"], in_const)
            for c in range(KC):
                dma(x[:, c], io["x"][:, c], in_x[c])
            dma(e_wpool[:, :, :], io["pool_w"], in_even)
            dma(e_vc[:, :], io["swa_v"], in_even)
            dma(e_rope[:, :, :], io["rope"], in_even)
            dma(e_kT[:, SEQ:SEQ + PAST], io["swa_k"], in_even)
            dma(e_u[:, :, PS + SEQ:2 * PS + SEQ], io["pool_past"], in_even)
            ac.wait_ge(in_const, 16)
            for c in range(KC):
                ac.wait_ge(in_x[c], 16)
                norm_hi(c, 0)
                if c >= 2:
                    ac.wait_ge(sum_add, c - 1)
                square(c, 0)
            rms(0, 0)

            for n in range(EVEN_IN):
                if n == 5:
                    ac.wait_ge(turned, 1)
                    ac.activation(e_v[:, 0:4], psum[:, 0, :].rearrange("p (t f) -> p t f", t=4), ACT.Copy)
                    ac.activation(e_v[0:SMP, 4], psum[0:SMP, 1, 0:P], ACT.Copy).then_inc(v_out, 1)
                if n >= 6:
                    g = n - 6
                    ac.wait_ge(side_mm, g + 1)
                    ac.activation(halves(y_hi[:, g]), pair((g + 1) % 2), ACT.Copy,
                                  scale=const("pool_scale")[:, g:g + 1]).then_inc(y_hi_done, 1)
            ac.wait_ge(evac, 4)
            dma(io["pool_new"][:, :, 0], e_u[:, :, SEQ:SEQ + PS], out_done)
            dma(io["pool_new"][:, :, 1], e_u[:, :, UE - PS:UE], out_done)
            ac.wait_ge(v_out, 1)
            dma(io["swa_v_new"][0], e_v[:, 3], out_done)
            dma(io["swa_v_new"][1, 0:P - SMP], e_vc[SMP:P, :], out_done)
            dma(io["swa_v_new"][1, P - SMP:P], e_v[0:SMP, 4], out_done)
            ac.wait_ge(rope_done, 1)
            dma(io["swa_k_new"][:, 0], e_kT[:, SEQ - P:SEQ], out_done)
            dma(io["swa_k_new"][:, 1], e_kT[:, KEYS - P:KEYS], out_done)

            def even_exp(u):
                b, g = EU[u]
                (_, nq), (_, nk), _ = even_block(b)
                sm = small[0:nq, u % 2]
                ac.wait_ge(negm, u + 1)
                if u >= 2:
                    ac.wait_ge(p_turned, u - 1)
                S = s_even(u)
                for j in range(4):
                    o(ac.activation(probs[u % 2][0:nq, j * 256:j * 256 + nk], S[0:nq, j, 0:nk], ACT.Exp,
                                    bias=sm[:, 4 + j:5 + j], scale=0.125, accum_out=sm[:, 8 + j:9 + j]))
                ac.activation(sm[:, 16:20], sm[:, 12:16], ACT.Exp).then_inc(e_ready, 1)

            def even_turned(u):
                b, g = EU[u]
                (_, nq), _, runs = even_block(b)
                ac.wait_ge(p_turned, u + 1)
                if u >= 2:
                    ac.wait_ge(o_ready, u - 1)
                for kb, (_, kn) in enumerate(runs):
                    ins = ac.activation(probsT[u % 2][0:kn, kb, 0:4 * nq], psum[0:kn, 2 * (u % 2) + kb, 0:4 * nq],
                                        ACT.Copy)
                ins.then_inc(pT_out, 1)

            even_exp(0)
            even_exp(1)
            even_turned(0)
            for u, (b, g) in enumerate(EU):
                if g == 1:
                    (q0, nq), _, _ = even_block(b)
                    ac.wait_ge(o_ready, u + 1)
                    ac.activation(h_hi[:, 4:8, q0:q0 + nq],
                                  psum[:, 4 + b % 2, 0:4 * nq].rearrange("p (j q) -> p j q", j=4),
                                  ACT.Copy).then_inc(y_hi_done, 1)
                if u + 1 < len(EU):
                    even_turned(u + 1)
                if u + 2 < len(EU):
                    even_exp(u + 2)
            out_norm(1, KC)
            ac.wait_ge(out_done, 16 * 7)
            ffn(0, 1, 2 * KC)

            ac.wait_ge(x_upd, 3 * KC)
            dma(o_wg[0:16, :], io["gate_w"], in_odd)
            dma(o_rope[:, :, :], io["rope"], in_odd)
            dma(o_lp[:, :], io["lambda"], in_odd)
            dma(o_s_in[:, :], io["state"], in_odd)
            dma(io["tails"][:, 0], tails[:, :, :], out_done)
            rms(2, 0)
            for n, kind in enumerate(ODD_CHUNKS):
                if kind == "cg":
                    ac.wait_ge(evac, EVEN_IN + n + 1)
                    ac.activation(o_sg[:, n - 13], o_sg[:, n - 13], ACT.Silu).then_inc(silu_in, 1)
                if n == 0:
                    ac.wait_ge(lam_sum, 1)
                    ac.activation(lam[:, 2:4], lam[:, 0:2], ACT.Exp).then_inc(lam_exp, 1)
                if n == 2:
                    for j in range(2):
                        gt = gate_tmp[j]
                        ac.wait_ge(gate_z, j + 1)
                        o(ac.activation(gt[:, 1], gt[:, 1], ACT.Exp, scale=-1.0))
                        o.wait()
                        ac.activation(gt[:, 1], gt[:, 1], ACT.Ln, bias=1.0).then_inc(gate_l, 1)
                if n == 3:
                    for j in range(2):
                        gt = gate_tmp[j]
                        ac.wait_ge(cum_ready, j + 1)
                        o(ac.activation(gt[:, 0], gt[:, 2], ACT.Exp, scale=1.0 / 16))
                        o(ac.activation(gt[:, 3], gt[:, 2], ACT.Exp, scale=-1.0 / 16))
                        ac.activation(gt[:, 1], gt[:, 1], ACT.Exp, scale=1.0 / 16).then_inc(decays, 1)
                if 6 <= n < 14:
                    dst, h = (o_cv, n - 6) if n < 10 else (o_dv, n - 10)
                    ac.wait_ge(turned, n - 4)
                    o(ac.activation(dst[:, 0:4, h * P:(h + 1) * P],
                                    psum[:, 0, :].rearrange("p (t f) -> p t f", t=4), ACT.Copy))
                    ac.activation(dst[0:SMP, 4, h * P:(h + 1) * P], psum[0:SMP, 1, 0:P], ACT.Copy).then_inc(v_out, 1)
                if n == 12:
                    ac.wait_ge(side_mm, 6)
                    ac.activation(o_kw[:, 0:4].rearrange("p (c t) f -> p c (t f)", c=2), psum[:, 2:4, :], ACT.Copy)\
                        .then_inc(v_out, 1)
                if n == 13:
                    ac.wait_ge(side_mm, 7)
                    ac.activation(o_kw[0:SMP, 4], psum[0:SMP, 2, 0:256], ACT.Copy).then_inc(v_out, 1)
                    ac.wait_ge(v_out, V_ALL)
                    dma(io["diff_v_new"][0:SEQ].rearrange("(t p) f -> p t f", p=P), o_dv[:, 0:4], out_done)
                    dma(io["diff_v_new"][SEQ:T], o_dv[0:SMP, 4], out_done)
                if n >= GLA_SLOT0:
                    k = n - GLA_SLOT0
                    t = (k - 1) // 2
                    if k % 2 == 1:
                        w = TILES[t][1]
                        ac.wait_ge(og_ready, t + 1)
                        if t >= 1:
                            ac.wait_ge(head_sum, t)
                        ac.activation(sq_h[:, 0:4 * w].rearrange("p (c n) -> p c n", c=2), psum[:, 2:4, 0:2 * w],
                                      ACT.Square).then_inc(hsq_ready, 1)
                    elif k >= 2:
                        c0, w = TILES[t]
                        ac.wait_ge(head_sum, t + 1)
                        o(ac.activation(r_h[:, 0:4 * w].rearrange("p (c n) -> p c n", c=2),
                                        psum[:, 2:4, 256:256 + 2 * w], ACT.Ln, bias=eps, scale=1.0 / P))
                        o.wait()
                        ac.activation(r_h[:, 0:4 * w], r_h[:, 0:4 * w], ACT.Exp, scale=-0.5).then_inc(hrms_ready, 1)
                        ac.wait_ge(head_y, t + 1)
                        ac.activation(y_hi[:, 0:4, c0:c0 + w], head_t[:, 0:4 * w].rearrange("p (e q) -> p e q", e=4),
                                      ACT.Copy).then_inc(y_hi_done, 1)
                if n == 14:
                    ac.wait_ge(gla_in, 2)
                    dma(d_kT[:, :, SEQ:SEQ + PAST], io["diff_k"], in_cache)
                    dma(d_vc[:, :], io["diff_v"], in_cache)
            dma(io["state_new"][:, 0], o_st[:, 0], out_done)
            dma(io["state_new"][:, 1], o_s_out[:, :], out_done)
            dma(io["diff_k_new"][:, :, 0:SEQ], d_kT[:, :, 0:SEQ], out_done)
            dma(io["diff_k_new"][:, :, SEQ:T], d_kT[:, :, SEQ + PAST:KEYS], out_done)

            def odd_exp(u):
                b, h = OU[u]
                (_, nq), (_, nk), _ = odd_block(b)
                sm = small[0:nq, u % 2]
                ac.wait_ge(negm, 10 + u + 1)
                if u >= 2:
                    ac.wait_ge(p_turned, 10 + u - 1)
                for c in range(2):
                    ins = ac.activation(probs[u % 2][0:nq, c * 512:c * 512 + nk], psum[0:nq, 2 * (u % 2) + c, 0:nk],
                                        ACT.Exp, bias=sm[:, 4 + c:5 + c], scale=0.125, accum_out=sm[:, 8 + c:9 + c])
                ins.then_inc(e_ready, 1)

            def odd_turned(u):
                b, h = OU[u]
                (q0, nq), _, runs = odd_block(b)
                ac.wait_ge(p_turned, 10 + u + 1)
                ac.wait_ge(o_ready, 10 + u - 1)
                bank = psum[:, 2 * (u % 2), :]
                if b < 4:
                    n = len(runs) * P
                    ac.activation(probsT[u % 2][:, 0, 0:n], bank[:, 0:n], ACT.Copy).then_inc(pT_out, 1)
                else:
                    ac.activation(probsT[u % 2][:, 0, 0:nq], bank[:, 0:nq], ACT.Copy)
                    ac.activation(probsT[u % 2][0:SMP, 0, nq:2 * nq], bank[0:SMP, nq:2 * nq], ACT.Copy)\
                        .then_inc(pT_out, 1)

            def head_squares(b):
                nq = TILES[b][1]
                ac.wait_ge(head_out, b + 1)
                ac.wait_ge(head_sum, 5 + b)
                ac.activation(sq_h[:, 0:4 * nq], head_t[:, 0:4 * nq], ACT.Square).then_inc(hsq_ready, 1)

            def head_rstd(b):
                nq = TILES[b][1]
                ac.wait_ge(head_sum, 5 + b + 1)
                o(ac.activation(r_h[:, 0:4 * nq], psum[:, 5, 0:4 * nq], ACT.Ln, bias=eps, scale=1.0 / P))
                o.wait()
                ac.activation(r_h[:, 0:4 * nq], r_h[:, 0:4 * nq], ACT.Exp, scale=-0.5).then_inc(hrms_ready, 1)

            def head_hi(b):
                q0, nq = TILES[b]
                ac.wait_ge(head_y, 5 + b + 1)
                ac.activation(h_hi[:, 4:8, q0:q0 + nq], head_t[:, 0:4 * nq].rearrange("p (h q) -> p h q", h=4),
                              ACT.Copy).then_inc(y_hi_done, 1)

            odd_exp(0)
            odd_exp(1)
            odd_turned(0)
            for u, (b, h) in enumerate(OU):
                if h == 3:
                    head_squares(b)
                if u + 1 < len(OU):
                    odd_turned(u + 1)
                if u + 2 < len(OU):
                    odd_exp(u + 2)
                if h == 0 and b >= 1:
                    head_rstd(b - 1)
                if h == 1 and b >= 1:
                    head_hi(b - 1)
            head_rstd(4)
            head_hi(4)
            out_norm(3, X_ODD + KC)
            ac.wait_ge(out_done, 16 * 14)
            ffn(1, 3, X_ODD + 2 * KC)
            dma(io["tails"][:, 1], tails[:, :, :], out_done)
            rms(4, 2)

        @block.vector
        def _(ve):
            o = Order(ve, vec)

            def clear_sum(n):
                if n:
                    ve.wait_ge(sum_ready, n)
                o(ve.memset(sumsq[:, :], 0.0))

            def add_square(c, n, i=0):
                ve.wait_ge(sq_ready, 4 * i + (KC * n + c + 1))
                ve.tensor_tensor(sumsq[:, :], sumsq[:, :], sq[:, c % 2], ALU.add).then_inc(sum_add, 1)

            def norm_low(c, n, i=None):
                ch = c if i is None else 4 * i + c
                ve.wait_ge(h_hi_done, KC * n + c + 1 if i is None else 4 * i + (KC * n + c + 1))
                if i is not None:
                    settle(ve)
                w = norm_w[:, n, c:c + 1] if i is None else norm_w[:, n, bass.ds(ch, 1)]
                ve.scalar_tensor_tensor(h_lo[:, ch], x[:, ch], w, h_hi[:, ch].bitcast(F32),
                                        ALU.mult, ALU.subtract).then_inc(h_ready, 1)

            def inverse_rms(n):
                ve.wait_ge(rms_ready, n + 1)
                o(ve.reciprocal(rstd[:, :], rstd[:, :]))
                o.wait()

            def grouped(dst, acc, gap):
                for src, c, w in pieces(acc):
                    at_ = c + gap + (gap if c >= SEQ else 0)
                    ins = ve.tensor_tensor(dst[:, at_:at_ + w], src, rstd[:, c:c + w], ALU.mult)
                return ins

            def add_out(slab, value, acc, m):
                ve.wait_ge(slab, value)
                ve.tensor_tensor(halves(x[:, m]), halves(x[:, m]), pair(acc), ALU.add).then_inc(x_upd, 1)

            def out_first(s0, m, mid0, upd0):
                if m >= 0:
                    add_out(slab_done if m % 2 else mid_done, (s0 if m % 2 else mid0) + m // 2 + 1, 3, m)

            def out_norm(s0, mid0, n):
                for m in range(KC):
                    add_out(slab_done if m % 2 else mid_done, (s0 + 4 if m % 2 else mid0 + 4) + m // 2 + 1, 2 + m % 2, m)
                    if m < 4:
                        norm_low(m, n)
                    ve.wait_ge(sum_add, KC * n + m)
                    add_square(m, n)
                for m in range(4, KC):
                    norm_low(m, n)

            def ffn(layer, n_norm, upd0):
                s0, d0, f0 = S_UP[layer], S_DOWN[layer], FC * layer

                def chunk(i, p):
                    f = 2 * i + p
                    one = slice(f, f + 1) if isinstance(i, int) else bass.ds(f, 1)
                    g, c = gate[p], conv[p]

                    def tap(j):
                        return conv_w[:, layer, one, j]

                    ve.wait_ge(slab_done, 4 * i + (s0 + 2 * p + 1))
                    if layer or not (isinstance(i, int) and i == 0):
                        ve.wait_ge(conv_ready, 2 * i + (f0 + p - 1))
                    settle(ve)
                    grouped(g, 2 * p, 2).then_inc(gate_out, 1)
                    ve.wait_ge(gate_out, 2 * i + (f0 + p + 1))
                    settle(ve)
                    ve.tensor_copy(g[:, SEQ + 2:SEQ + 4].unsqueeze(1), conv_past[:, layer, one, :]).then_inc(vec, 1)
                    ve.tensor_copy(tails[:, one, 0:2], g[:, SEQ:SEQ + 2].unsqueeze(1)).then_inc(vec, 1)
                    ve.tensor_copy(tails[:, one, 2:4], g[:, GE - 2:GE].unsqueeze(1)).then_inc(vec, 1)
                    at_ = 10 * i + (vec0 + 5 * p)
                    ve.wait_ge(vec, at_ + 3)
                    ve.tensor_scalar(c[:, :], g[:, 0:CO], tap(0), None, ALU.mult).then_inc(vec, 1)
                    ve.wait_ge(vec, at_ + 4)
                    ve.scalar_tensor_tensor(c[:, :], g[:, 1:1 + CO], tap(1), c[:, :], ALU.mult, ALU.add)\
                        .then_inc(vec, 1)
                    ve.wait_ge(vec, at_ + 5)
                    ve.scalar_tensor_tensor(c[:, :], g[:, 2:2 + CO], tap(2), c[:, :], ALU.mult, ALU.add)\
                        .then_inc(conv_ready, 1)
                    ve.wait_ge(slab_done, 4 * i + (s0 + 2 * p + 2))
                    if layer or not (isinstance(i, int) and i == 0):
                        ve.wait_ge(y_ready, 2 * i + (f0 + p - 1))
                    ve.tensor_tensor(halves(sq[:, p]), pair(2 * p + 1), halves(rstd), ALU.mult).then_inc(val_out, 1)
                    ve.wait_ge(val_out, 2 * i + (f0 + p + 1))
                    ve.wait_ge(gelu_ready, 2 * i + (f0 + p + 1))
                    ve.tensor_tensor(sq[:, p, 0:SEQ], sq[:, p, 0:SEQ], c[:, 0:SEQ], ALU.mult)
                    ve.tensor_tensor(sq[:, p, SEQ:T], sq[:, p, SEQ:T], c[:, SEQ + 2:CO], ALU.mult).then_inc(y_f, 1)
                    ve.wait_ge(ffn_hi, 2 * i + (f0 + p + 1))
                    settle(ve)
                    ve.tensor_tensor(y_lo[:, f], sq[:, p], y_hi[:, f].bitcast(F32), ALU.subtract).then_inc(y_ready, 1)

                for p in range(2):
                    o(ve.memset(gate[p][:, 0:2], 0.0))
                ve.wait_ge(sum_add, KC * (n_norm + 1))
                inverse_rms(n_norm)
                vec0 = o.n[vec.name]
                for p in range(2):
                    chunk(0, p)
                with ve.Fori(1, FC // 2) as i:
                    for p in range(2):
                        chunk(i, p)
                o.n[vec.name] += 5 * FC
                clear_sum(n_norm + 1)
                o.wait()
                with ve.Fori(0, 2) as i:
                    for j in range(4):
                        ve.wait_ge(slab_done, 12 * i + (d0 + 3 * j + 3))
                        ve.tensor_tensor(halves(x[:, 4 * i + j]), halves(x[:, 4 * i + j]), pair(j % 2),
                                         ALU.add).then_inc(x_upd, 1)
                        if n_norm < 3:
                            norm_low(j, n_norm + 1, i)
                        ve.wait_ge(sum_add, 4 * i + (KC * (n_norm + 1) + j))
                        add_square(j, n_norm + 1, i)

            clear_sum(0)
            o(ve.memset(mask_q[:, :, :], 0.0))
            o(ve.memset(mask_k[:, :], 0.0))
            o.wait()
            for r in (0, 64):
                o(ve.memset(mask_q[r:r + 1, 0, 0:CHUNK], 1.0))
                o(ve.memset(mask_q[r:r + 1, 1, CHUNK:P], 1.0))
                o(ve.memset(mask_k[r:r + 1, :], NEG))
            o(ve.memset(e_u[:, :, 0:PS], 0.0))
            ve.nop().then_inc(setup, 1)
            for c in range(KC):
                norm_low(c, 0)
                if c:
                    ve.wait_ge(sum_add, c)
                add_square(c, 0)
            inverse_rms(0)

            def scale_rope(rope):
                for k in range(2):
                    o(ve.tensor_tensor(rope[:, k], rope[:, k], rstd[:, :], ALU.mult))

            def rotate(acc, z, swapped, rope, kT, qT_dst):
                o(ve.stream_shuffle(halves(swapped), pair(acc), PARTNER))
                o(ve.tensor_tensor(halves(z), pair(acc), halves(rope[:, 0]), ALU.mult), evac)
                o.wait()
                o(ve.tensor_tensor(swapped, swapped, rope[:, 1], ALU.mult))
                o.wait()
                if kT is None:
                    o(ve.tensor_tensor(qT_dst, z, swapped, ALU.add), rope_done)
                else:
                    o(ve.tensor_tensor(kT[:, 0:SEQ], z[:, 0:SEQ], swapped[:, 0:SEQ], ALU.add))
                    o(ve.tensor_tensor(kT[:, SEQ + PAST:KEYS], z[:, SEQ:T], swapped[:, SEQ:T], ALU.add), rope_done)

            for n in range(EVEN_IN):
                ve.wait_ge(slab_done, n + 1)
                if n < 4:
                    o(grouped(e_u[:, n], 2 + n % 2, PS), evac)
                elif n == 4:
                    o(ve.tensor_tensor(halves(e_vT), pair(2), halves(rstd), ALU.mult), evac)
                    scale_rope(e_rope)
                if n < 4:
                    if n == 0:
                        ve.wait_ge(in_even, 16 * NEVEN)
                    u, w = e_u[:, n], 1
                    src, k = u, 0
                    while w < POOL_W[n]:
                        dst = e_w[:, k % 2]
                        lo = 2 * w - 1
                        o.wait()
                        o(ve.tensor_tensor(dst[:, lo:UE], src[:, lo:UE], src[:, lo - w:UE - w], ALU.add))
                        src, w, k = dst, 2 * w, k + 1
                    o.wait()
                    o(ve.scalar_tensor_tensor(e_diff[:, n, 0:SEQ], src[:, PS:PS + SEQ], 1.0 / w, u[:, PS:PS + SEQ],
                                              ALU.mult, ALU.subtract))
                    o(ve.scalar_tensor_tensor(e_diff[:, n, SEQ:T], src[:, UE - SMP:UE], 1.0 / w, u[:, UE - SMP:UE],
                                              ALU.mult, ALU.subtract))
                    o.wait()
                    o(ve.tensor_tensor(e_diff[:, n, 0:16], src[:, PS:PS + 16],
                                       const("inv_count")[:, 16 * n:16 * n + 16], ALU.mult))
                    o.wait()
                    o(ve.tensor_tensor(e_diff[:, n, 0:16], e_diff[:, n, 0:16], u[:, PS:PS + 16], ALU.subtract),
                      diff_ready)
                if n >= 5:
                    o.wait()
                    rotate(2 + n % 2, ez[:, n % 2], e_swap[:, :], e_rope, e_kT if n == 5 else None, e_qT[:, max(n - 6, 0)])
                if n >= 6:
                    g = n - 6
                    ve.wait_ge(y_hi_done, g + 1)
                    o(ve.scalar_tensor_tensor(halves(y_lo[:, g]), pair((g + 1) % 2), const("pool_scale")[:, g:g + 1],
                                              halves(y_hi[:, g]).bitcast(F32), ALU.mult, ALU.subtract), y_lo_done)

            def even_max(u):
                b, g = EU[u]
                (_, nq), (_, nk), _ = even_block(b)
                sm = small[0:nq, u % 2]
                sink = const("sinks")[0:nq, 4 * g:4 * g + 4]
                ve.wait_ge(s_ready, u + 1)
                o(ve.tensor_reduce(sm[:, 0:4], s_even(u)[0:nq, :, 0:nk], AX.X, ALU.max))
                o.wait()
                o(ve.scalar_tensor_tensor(sm[:, 0:4], sm[:, 0:4], 0.125, sink, ALU.mult, ALU.max))
                o.wait()
                o(ve.tensor_scalar(sm[:, 4:8], sm[:, 0:4], -1.0, None, ALU.mult))
                o(ve.tensor_tensor(sm[:, 12:16], sink, sm[:, 0:4], ALU.subtract), negm)

            def even_normalise(u):
                b, g = EU[u]
                (_, nq), (_, nk), _ = even_block(b)
                sm = small[0:nq, u % 2]
                ve.wait_ge(e_ready, u + 1)
                o(ve.tensor_tensor(sm[:, 20:24], sm[:, 8:12], sm[:, 16:20], ALU.add))
                o.wait()
                o(ve.reciprocal(sm[:, 20:24], sm[:, 20:24]))
                o.wait()
                pr = probs[u % 2][0:nq, :].rearrange("p (h k) -> p h k", h=4)[:, :, 0:nk]
                o(ve.tensor_tensor(pr, pr, sm[:, 20:24].unsqueeze(2).broadcast_to([nq, 4, nk]), ALU.mult), p_norm)

            def low(b, src):
                (q0, nq), _, _ = odd_block(b)
                o(ve.tensor_tensor(h_lo[:, 4:8, q0:q0 + nq], src, h_hi[:, 4:8, q0:q0 + nq].bitcast(F32),
                                   ALU.subtract), y_lo_done)

            def even_low(b):
                (_, nq), _, _ = even_block(b)
                ve.wait_ge(y_hi_done, 4 + b + 1)
                low(b, psum[:, 4 + b % 2, 0:4 * nq].rearrange("p (j q) -> p j q", j=4))

            even_max(0)
            even_max(1)
            even_normalise(0)
            for u, (b, g) in enumerate(EU):
                if u + 1 < len(EU):
                    even_normalise(u + 1)
                if u < KC:
                    out_first(S_EVEN_OUT, u, 0, 0)
                if g == 0 and b >= 1:
                    even_low(b - 1)
                if u + 2 < len(EU):
                    even_max(u + 2)
            even_low(4)
            clear_sum(1)
            o.wait()
            out_norm(S_EVEN_OUT, 0, 1)
            ve.wait_ge(out_done, 16 * 7)
            ffn(0, 1, 2 * KC)
            inverse_rms(2)
            ve.wait_ge(in_odd, 16 * NODD)
            lp = o_lp[:, :].rearrange("p (a b d) -> p a b d", a=2, b=2)
            o(ve.tensor_tensor(lp[:, :, 0], lp[:, :, 0], lp[:, :, 1], ALU.mult))
            o.wait()
            o(ve.tensor_reduce(lam[:, 0:2], lp[:, :, 0], AX.X, ALU.add), lam_sum)
            o(ve.tensor_scalar(dnorm[:, :], const("diff_norm"), 1.0 - LAMBDA_INIT, None, ALU.mult))
            ve.wait_ge(lam_exp, 1)
            o(ve.tensor_tensor(lam[:, 4:5], lam[:, 2:3], lam[:, 3:4], ALU.subtract))
            o.wait()
            o(ve.tensor_scalar(lam[:, 5:6], lam[:, 4:5], LAMBDA_INIT, None, ALU.add))
            state_n = [0]
            for n, kind in enumerate(ODD_CHUNKS):
                acc = 2 + n % 2
                src = pair(acc)
                ve.wait_ge(slab_done, S_ODD_IN + n + 1)
                if kind == "cr":
                    o(ve.tensor_tensor(halves(o_cr[0:16, :]), src[0:16], halves(rstd[0:16, :]), ALU.mult), evac)
                elif kind == "cq":
                    o(ve.scalar_tensor_tensor(halves(o_q[:, n - 1]), src, 0.125, halves(rstd), ALU.mult, ALU.mult), evac)
                elif kind == "ck":
                    o(ve.tensor_tensor(halves(o_k[:, n - 3]), src, halves(rstd), ALU.mult), evac)
                elif kind == "cg":
                    o(ve.tensor_tensor(halves(o_sg[:, n - 13]), src, halves(rstd), ALU.mult), evac)
                elif n < 17:
                    if n >= 7:
                        ve.wait_ge(turned, n - 5)
                    o(ve.tensor_tensor(halves(oz[:, n % 2]), src, halves(rstd), ALU.mult), evac)
                if n == 5:
                    scale_rope(o_rope)
                if n == 1:
                    o.wait()
                    o(ve.memset(resets, 1.0))
                    o.wait()
                    o(ve.memset(resets[:, 0:SEQ].rearrange("p (n c) -> p n c", c=CHUNK)[:, :, 0:1], 0.0))
                    o(ve.memset(resets[:, SEQ:SEQ + 1], 0.0))
                    o(ve.memset(o_st[:, 0], 0.0))
                    ve.wait_ge(side_mm, 5)
                    for j in range(2):
                        gt = gate_tmp[j]
                        o(ve.tensor_scalar(halves(gt[:, 0]), pair(j), const("b_gate")[:, j:j + 1], None, ALU.add))
                        o.wait()
                        o(ve.scalar_tensor_tensor(gt[:, 1], gt[:, 0], -1.0, gt[:, 0], ALU.mult, ALU.max), gate_z)
                if n == 2:
                    for j in range(2):
                        gt = gate_tmp[j]
                        ve.wait_ge(gate_l, j + 1)
                        o(ve.scalar_tensor_tensor(gt[:, 0], gt[:, 0], 0.0, gt[:, 1], ALU.min, ALU.subtract))
                        o.wait()
                        o(ve.tensor_tensor_scan(gt[:, 2], resets, gt[:, 0], 0.0, ALU.mult, ALU.add))
                        o.wait()
                        for c0, nc_, w in ((0, SEQ // CHUNK, CHUNK), (SEQ, 1, SMP)):
                            cum = gt[:, 2, c0:c0 + nc_ * w].rearrange("p (n c) -> p n c", c=w)
                            last = cum[:, :, w - 1:w].broadcast_to([P, nc_, w])
                            ins = ve.tensor_tensor(gt[:, 1, c0:c0 + nc_ * w].rearrange("p (n c) -> p n c", c=w),
                                                   last, cum, ALU.subtract)
                            o(ins, cum_ready if c0 else None)
                if n == 4:
                    o.wait()
                    for j in range(2):
                        gt = gate_tmp[j]
                        ve.wait_ge(decays, j + 1)
                        o(ve.tensor_copy(elast[:, j, 0:8].unsqueeze(2),
                                         gt[:, 0, 0:SEQ].rearrange("p (n c) -> p n c", c=CHUNK)[:, :, CHUNK - 1:CHUNK]))
                        o(ve.tensor_copy(elast[:, j, 8:9], gt[:, 0, T - 1:T]))
                        o(ve.tensor_tensor(o_q[:, j], o_q[:, j], gt[:, 0], ALU.mult))
                        o(ve.tensor_tensor(o_kd[:, j], o_k[:, j], gt[:, 3], ALU.mult))
                        o.wait()
                        o(ve.tensor_tensor(o_k[:, j], o_k[:, j], gt[:, 1], ALU.mult), gla_in)
                if n >= 17:
                    h = (n - 17) % 4
                    o.wait()
                    if n < 19:
                        ve.wait_ge(turned, 9)
                    rotate(acc, oz[:, n % 2], o_swap[:, :], o_rope, d_kT[:, h] if n < 21 else None, d_qT[:, h])
                if n >= GLA_SLOT0:
                    k = n - GLA_SLOT0
                    if k % 2 == 0:
                        if k >= 2:
                            t = k // 2 - 1
                            c0, w = TILES[t]
                            ve.wait_ge(hrms_ready, t + 1)
                            o(ve.tensor_tensor(head_t[:, 0:4 * w], head_t[:, 0:4 * w], r_h[:, 0:4 * w], ALU.mult))
                            ve.wait_ge(silu_in, 4)
                            o.wait()
                            heads = head_t[:, 0:4 * w].rearrange("p (e q) -> p e q", e=4)
                            o(ve.tensor_tensor(heads, heads, o_sg[:, :, c0:c0 + w], ALU.mult), head_y)
                            ve.wait_ge(y_hi_done, 9 + t + 1)
                            o(ve.tensor_tensor(y_lo[:, 0:4, c0:c0 + w], head_t[:, 0:4 * w].rearrange("p (e q) -> p e q", e=4),
                                               y_hi[:, 0:4, c0:c0 + w].bitcast(F32), ALU.subtract), y_lo_done)
                        t = k // 2
                        if t < 5:
                            c0, w = TILES[t]
                            ve.wait_ge(att_ready, t + 1)
                            o.wait()
                            o(ve.tensor_tensor(att_m[0:w, 0:4 * w].rearrange("k (p j q) -> k p j q", p=2, j=2),
                                               psum[0:w, 0:2, 0:2 * w].rearrange("k p (j q) -> k p j q", j=2),
                                               causal[0:w, 0:w].unsqueeze(1).unsqueeze(1).broadcast_to([w, 2, 2, w]),
                                               ALU.mult), att_out)
                            for cc in range(2 if t < 4 else 1):
                                n_ = 2 * t + cc
                                s_in = o_s_in if t == 4 else o_st[:, n_ % 4]
                                s_out = o_s_out if t == 4 else o_st[:, (n_ + 1) % 4]
                                o.wait()
                                for j in range(2):
                                    cols = slice(j * P, (j + 1) * P)
                                    o(ve.scalar_tensor_tensor(s_out[:, cols], s_in[:, cols], elast[:, j, n_:n_ + 1],
                                                              psum[:, cc, 256 + j * P:256 + (j + 1) * P],
                                                              ALU.mult, ALU.add), st_ready if j else None)
                    else:
                        t = (k - 1) // 2
                        c0, w = TILES[t]
                        ve.wait_ge(og_ready, t + 1)
                        ve.wait_ge(hsq_ready, t + 1)
                        if t >= 1:
                            ve.wait_ge(y_lo_done, 9 + t)
                        o(ve.tensor_scalar(head_t[:, 0:4 * w].rearrange("p (c n) -> p c n", c=2),
                                           psum[:, 2:4, 0:2 * w], const("gla_norm"), None, ALU.mult), og_read)

            def odd_max(u):
                b, h = OU[u]
                (_, nq), (_, nk), _ = odd_block(b)
                sm = small[0:nq, u % 2]
                ve.wait_ge(s_ready, 10 + u + 1)
                o(ve.tensor_reduce(sm[:, 0:2], psum[0:nq, 2 * (u % 2):2 * (u % 2) + 2, 0:nk], AX.X, ALU.max))
                o.wait()
                o(ve.tensor_scalar(sm[:, 4:6], sm[:, 0:2], -0.125, None, ALU.mult), negm)

            def odd_normalise(u):
                b, h = OU[u]
                (_, nq), (_, nk), _ = odd_block(b)
                sm = small[0:nq, u % 2]
                ve.wait_ge(e_ready, 10 + u + 1)
                o(ve.reciprocal(sm[:, 20:22], sm[:, 8:10]))
                o.wait()
                o(ve.tensor_tensor(sm[:, 22:23], sm[:, 21:22], lam[0:nq, 5:6], ALU.mult))
                o.wait()
                p0, p1 = probs[u % 2][0:nq, 0:nk], probs[u % 2][0:nq, 512:512 + nk]
                o(ve.tensor_scalar(p1, p1, sm[:, 22:23], None, ALU.mult))
                o.wait()
                o(ve.scalar_tensor_tensor(p0, p0, sm[:, 20:21], p1, ALU.mult, ALU.subtract), p_norm)

            def head_copy(b):
                nq = TILES[b][1]
                ve.wait_ge(o_ready, 10 + 4 * b + 4)
                ve.wait_ge(y_lo_done, 14 + b)
                o(ve.tensor_copy(head_t[:, 0:4 * nq], psum[:, 4, 0:4 * nq]), head_out)

            def head_scale(b):
                nq = TILES[b][1]
                ve.wait_ge(hrms_ready, 5 + b + 1)
                o(ve.scalar_tensor_tensor(head_t[:, 0:4 * nq], head_t[:, 0:4 * nq], dnorm[:, :], r_h[:, 0:4 * nq],
                                          ALU.mult, ALU.mult), head_y)

            def head_low(b):
                nq = TILES[b][1]
                ve.wait_ge(y_hi_done, 14 + b + 1)
                low(b, head_t[:, 0:4 * nq].rearrange("p (h q) -> p h q", h=4))

            odd_max(0)
            odd_max(1)
            odd_normalise(0)
            for u, (b, h) in enumerate(OU):
                if u + 1 < len(OU):
                    odd_normalise(u + 1)
                if h == 1 and b >= 1:
                    head_scale(b - 1)
                if h == 2 and b >= 1:
                    head_low(b - 1)
                if u % 2 == 0 and u // 2 < KC:
                    out_first(S_ODD_OUT, u // 2, KC, 0)
                if h == 3:
                    head_copy(b)
                if u + 2 < len(OU):
                    odd_max(u + 2)
            head_scale(4)
            head_low(4)
            ve.wait_ge(head_sum, 10)
            o(ve.memset(sumsq[:, :], 0.0))
            o.wait()
            out_norm(S_ODD_OUT, KC, 3)
            ve.wait_ge(out_done, 16 * 14)
            ffn(1, 3, X_ODD + 2 * KC)

            ve.wait_ge(rms_ready, 5)
            o(ve.reciprocal(rstd[:, :], rstd[:, :]))
            o.wait()
            for c in range(KC):
                ve.scalar_tensor_tensor(x[:, c], x[:, c], norm_w[:, 4, c:c + 1], rstd[:, :],
                                        ALU.mult, ALU.mult).then_inc(y_out, 1)


_INS = {"x": (P, KC, T), "weights": (NSLAB, P, 1024), "consts": (P, NCONST), "pool_w": (P, 4, P),
        "swa_v": (P, P), "rope": (P, 2, T), "swa_k": (P, P), "pool_past": (P, 4, PS), "gate_w": (16, 256),
        "lambda": (P, 256), "state": (P, 256), "diff_k": (P, 4, P), "diff_v": (P, 512)}
_OUTS = {"y": (P, KC * T), "pool_new": (P, 4, 2, PS), "swa_v_new": (2, P, P), "swa_k_new": (P, 2, P),
         "state_new": (P, 2, 256), "diff_k_new": (P, 4, T), "diff_v_new": (T, 512), "tails": (P, 2, FC, 4)}


def lay_out(i):
    f = {k: np.asarray(v) for k, v in i.items()}
    out = {}
    tok = np.concatenate([f["x_prompt"][0], f["x_sample"][0]])
    out["x"] = np.ascontiguousarray(tok.T.reshape(KC, P, T).transpose(1, 0, 2))

    w = np.zeros((NSLAB, P, KC, P), np.float32)

    def columns(m):
        return m.reshape(m.shape[0] // P, P, m.shape[1] // P, P).transpose(2, 1, 0, 3)

    e = f["even_w_in"][0]
    q = e[:, 512:1024].reshape(D, 2, 4, 64).transpose(0, 2, 1, 3).reshape(D, 512)
    w[0:EVEN_IN] = columns(np.concatenate([e[:, 0:512], e[:, 1152:1280], e[:, 1024:1152], q], 1))

    def out_slabs(m, s):
        for half in range(2):
            t = m[512 * half:512 * (half + 1)].reshape(4, P, 4, 2, P)
            w[s + 4 * half:s + 4 * half + 4] = t.transpose(2, 1, 3, 0, 4).reshape(4, P, KC, P)

    eo = f["even_w_out"][0]
    eo = np.concatenate([eo[0:512], eo[512:].reshape(2, 4, 64, D).transpose(1, 0, 2, 3).reshape(512, D)])
    out_slabs(eo, S_EVEN_OUT)
    oi = f["odd_w_in"][0]
    swap = [0, 2, 1, 3]
    heads = lambda m: m.reshape(D, 4, P)[:, swap].reshape(D, 512)
    cr = np.zeros((D, P), np.float32)
    cr[:, 0:16] = oi[:, 1536:1552]
    w[S_ODD_IN:S_ODD_OUT] = columns(np.concatenate(
        [cr, oi[:, 0:512], heads(oi[:, 512:1024]), oi[:, 2576:3088], heads(oi[:, 1024:1536]),
         oi[:, 2064:2576], oi[:, 1552:2064]], 1))
    oo = f["odd_w_out"][0]
    out_slabs(np.concatenate([oo[0:512].reshape(4, P, D)[swap].reshape(512, D), oo[512:]]), S_ODD_OUT)
    for n in range(2):
        up = columns(f["ffn_w_up"][n])
        w[S_UP[n]:S_UP[n] + UP:2] = up[0:FC]
        w[S_UP[n] + 1:S_UP[n] + UP:2] = up[FC:]
        down = columns(f["ffn_w_down"][n])
        for part in range(DOWN_PARTS):
            k = min(8, FC - 8 * part)
            w[S_DOWN[n] + part:S_DOWN[n] + DOWN:DOWN_PARTS, :, 0:k] = down[:, :, 8 * part:8 * part + k]
    out["weights"] = w.reshape(NSLAB, P, 1024)

    c = np.zeros((P, NCONST), np.float32)

    def put(name, v):
        c[:, COLS[name][0]:COLS[name][1]] = v

    def chunked(v):
        return v.reshape(-1, P).T

    put("ident", np.eye(P))
    put("ones", 1.0)
    r = np.arange(P)
    put("causal", (r[:, None] <= r[None]) & (r[:, None] // CHUNK == r[None] // CHUNK))
    norms = [f["norm_mix_w"][0], f["norm_ffn_w"][0], f["norm_mix_w"][1], f["norm_ffn_w"][1], f["final_norm_w"]]
    put("norm", chunked(np.stack(norms)))
    put("conv_w", f["ffn_conv_w"].reshape(2, 3, FC, P).transpose(3, 0, 2, 1).reshape(P, -1))
    put("conv_b", chunked(f["ffn_conv_b"]))
    put("conv_past", f["cache_ffn_conv"][:, 0].reshape(2, 2, FC, P).transpose(3, 0, 2, 1).reshape(P, -1))
    put("pool_scale", chunked(f["pool_scale"][0]))
    put("sinks", np.broadcast_to(f["swa_sinks"][0], (P, 8)))
    put("b_gate", chunked(f["gla_b_gate"][0]))
    put("gla_norm", chunked(f["gla_norm_w"][0]))
    put("diff_norm", chunked(f["diff_norm_w"][0]))
    put("eps", EPS)
    put("inv_count", np.concatenate([1.0 / np.minimum(g, np.arange(16) + 1) for g in POOL_W]))
    out["consts"] = c

    out["pool_w"] = np.ascontiguousarray(f["pool_w"][0].transpose(1, 0, 2))
    out["swa_v"] = f["cache_swa_v"][0, 0].reshape(PAST, P)
    out["swa_k"] = np.ascontiguousarray(f["cache_swa_k"][0, 0].reshape(PAST, P).T)
    out["pool_past"] = np.ascontiguousarray(f["cache_pool"][0, 0].T.reshape(4, P, PS).transpose(1, 0, 2))
    pos = np.concatenate([np.arange(SEQ), PAST + np.arange(SMP)]).astype(np.float32)
    half = ROT // 2
    inv = np.exp(np.float32(-math.log(THETA)) * np.arange(half, dtype=np.float32) * np.float32(2.0 / ROT))
    ang = (pos[None] * inv.astype(np.float32)[:, None]).astype(np.float32)
    rope = np.zeros((2, 64, 2, T), np.float32)
    rope[:, :, 0] = 1.0
    rope[:, 0:half, 0] = rope[:, half:ROT, 0] = np.cos(ang)
    rope[:, 0:half, 1] = -np.sin(ang)
    rope[:, half:ROT, 1] = np.sin(ang)
    out["rope"] = rope.reshape(P, 2, T)
    out["gate_w"] = f["gla_w_gate2"][0]
    out["lambda"] = np.ascontiguousarray(np.broadcast_to(f["diff_lambda"][0].reshape(1, 256), (P, 256)))
    out["state"] = np.ascontiguousarray(f["state_gla"][0, 0].reshape(2, P, P).transpose(1, 0, 2)).reshape(P, 256)
    out["diff_k"] = np.ascontiguousarray(f["cache_diff_k"][0, 0].reshape(PAST, 4, P).transpose(2, 1, 0))
    out["diff_v"] = f["cache_diff_v"][0, 0].reshape(PAST, 512)
    return out


def take_out(r):
    y = r["y"].reshape(P, KC, T).transpose(2, 1, 0).reshape(T, D)
    pool = r["pool_new"].transpose(2, 3, 1, 0).reshape(2, 1, 1, PS, 512)
    k = r["swa_k_new"].transpose(1, 2, 0).reshape(2, 1, 1, P, 2, 64)
    v = r["swa_v_new"].reshape(2, 1, 1, P, 2, 64)
    st = r["state_new"].reshape(P, 2, 2, P).transpose(1, 2, 0, 3).reshape(2, 1, 1, 4, 64, P)
    dk = r["diff_k_new"].transpose(2, 1, 0).reshape(T, 4, 2, 64)
    dv = r["diff_v_new"].reshape(T, 4, P)
    ffn = r["tails"].reshape(P, 2, FC, 2, 2).transpose(3, 1, 4, 2, 0).reshape(2, 2, 1, 2, FF)

    def g(n):
        s = slice(0, SEQ) if n == 0 else slice(SEQ, T)
        return (pool[n], k[n], v[n], st[n], dk[s][None, None], dv[s][None, None], ffn[n])

    return tuple(np.ascontiguousarray(a) for a in (y[None, 0:SEQ], y[None, SEQ:T], *g(0), *g(1)))


def kernel(**inputs):
    import concourse.bacc as bacc
    from concourse.bass_utils import run_bass_kernel_spmd

    nc = bacc.Bacc("TRN2", target_bir_lowering=False, num_devices=1)
    arrays = lay_out(inputs)
    io = {n: nc.dram_tensor(f"in_{n}", s, F32, kind="ExternalInput").ap() for n, s in _INS.items()}
    io |= {n: nc.dram_tensor(f"out_{n}", s, F32, kind="ExternalOutput").ap() for n, s in _OUTS.items()}
    build(nc, io)
    r = run_bass_kernel_spmd(nc, [{f"in_{n}": arrays[n] for n in _INS}], core_ids=[0])
    return take_out({n: r.results[0][f"out_{n}"] for n in _OUTS})
```
